# Optimizing a Trainium2 kernel written in Bass

```python
import math
import jax, jax.numpy as jnp
from jax import lax
import numpy as np

D_MODEL = 1024
BATCH = 1
SEQ = 256
DEPTH = 2

N_HEADS = 16
HEAD_DIM = D_MODEL // N_HEADS
ROPE_THETA = 10000.0
N_MIXERS = 2
DN_ALPHA = (2 * DEPTH) ** 0.25
DN_BETA = (8 * DEPTH) ** -0.25
LN_EPS = 1e-5
NEG = -1e30
FORCE = 1e9

NSA_KV_GROUPS = 4
NSA_HPG = N_HEADS // NSA_KV_GROUPS
NSA_KV_DIM = NSA_KV_GROUPS * HEAD_DIM
NSA_CMP_LEN = 32
NSA_CMP_STRIDE = 16
NSA_CMP_HIDDEN = 256
NSA_SEL_BLOCK = 64
NSA_SEL_TOPN = 16
NSA_WINDOW = 512
NSA_QB = 64
NSA_IN_DIM = D_MODEL + 6 * NSA_KV_DIM + 3 * N_HEADS

MOBA_BLOCK = 256
MOBA_TOPK = 3
MOBA_QB = 16
MOBA_IN_DIM = 3 * D_MODEL

N_EXPERTS = 16
N_GROUPS = 4
EXPERTS_PER_GROUP = N_EXPERTS // N_GROUPS
TOP_K = 2
D_EXPERT = 512

N_NSA_LAYERS = (DEPTH + 1) // 2
N_MOBA_LAYERS = DEPTH // 2

kernel_name = 'nsa_moba_interleaved_grouped_moe_deepnorm'

def layer_norm(x, g, b):
    xf = x.astype(jnp.float32)
    mu = xf.mean(-1, keepdims=True)
    var = jnp.mean(jnp.square(xf - mu), -1, keepdims=True)
    return ((xf - mu) * lax.rsqrt(var + LN_EPS) * g.astype(jnp.float32) + b.astype(jnp.float32)).astype(x.dtype)

def rope_tables(pos):
    inv = 1.0 / (ROPE_THETA ** (jnp.arange(0, HEAD_DIM, 2, dtype=jnp.float32) / HEAD_DIM))
    ang = pos.astype(jnp.float32)[:, None] * inv[None, :]
    return jnp.cos(ang), jnp.sin(ang)

def apply_rope(x, cos, sin):
    x1, x2 = jnp.split(x.astype(jnp.float32), 2, axis=-1)
    return jnp.concatenate([x1 * cos - x2 * sin, x2 * cos + x1 * sin], axis=-1).astype(x.dtype)

def _split_heads(t, n):
    B, S, _ = t.shape
    return t.reshape(B, S, n, HEAD_DIM).transpose(0, 2, 1, 3)

def _merge_chunks(o):
    nc, B, H, qb, dh = o.shape
    return o.transpose(1, 0, 3, 2, 4).reshape(B, nc * qb, H * dh)

def nsa_mixer(h, w_in, w_out, cmp_k_w1, cmp_k_w2, cmp_v_w1, cmp_v_w2, cmp_k_pos, cmp_v_pos):
    B, S, _ = h.shape
    G, HPG, dh = NSA_KV_GROUPS, NSA_HPG, HEAD_DIM
    L, STR, SB, W, QB = NSA_CMP_LEN, NSA_CMP_STRIDE, NSA_SEL_BLOCK, NSA_WINDOW, NSA_QB
    n_cmp = (S - L) // STR + 1
    n_sel = S // SB
    top_n = min(NSA_SEL_TOPN, n_sel)
    scale = dh ** -0.5

    proj = h @ w_in
    splits = np.cumsum([D_MODEL] + [NSA_KV_DIM] * 6).tolist()
    q, kc_raw, vc_raw, ks, vs, kw, vw, gates = jnp.split(proj, splits, axis=-1)

    cos, sin = rope_tables(jnp.arange(S))
    q = apply_rope(_split_heads(q, N_HEADS), cos, sin).reshape(B, G, HPG, S, dh)
    ks = apply_rope(_split_heads(ks, G), cos, sin)
    kw = apply_rope(_split_heads(kw, G), cos, sin)
    vs = _split_heads(vs, G)
    vw = _split_heads(vw, G)

    win_idx = jnp.arange(n_cmp)[:, None] * STR + jnp.arange(L)[None, :]
    cmp_end = win_idx[:, -1]

    def compress(t, pos_emb, w1, w2):
        blocks = _split_heads(t, G)[:, :, win_idx] + pos_emb
        return jax.nn.gelu(blocks.reshape(B, G, n_cmp, L * dh) @ w1) @ w2

    ccos, csin = rope_tables(cmp_end)
    kc = apply_rope(compress(kc_raw, cmp_k_pos, cmp_k_w1, cmp_k_w2), ccos, csin)
    vc = compress(vc_raw, cmp_v_pos, cmp_v_w1, cmp_v_w2)

    ci = jnp.arange(n_cmp)[:, None]
    sj = jnp.arange(n_sel)[None, :]
    overlap = ((ci * STR < (sj + 1) * SB) & (ci * STR + L > sj * SB)).astype(jnp.float32)

    ks_blk = ks.reshape(B, G, n_sel, SB, dh)
    vs_blk = vs.reshape(B, G, n_sel, SB, dh)
    pad = ((0, 0), (0, 0), (W, 0), (0, 0))
    kw_pad = jnp.pad(kw, pad)
    vw_pad = jnp.pad(vw, pad)
    bi = jnp.arange(B)[:, None, None, None]
    gi = jnp.arange(G)[None, :, None, None]
    blk_ids = jnp.arange(n_sel)

    def chunk(c):
        s0 = c * QB
        tq = s0 + jnp.arange(QB)
        qc = lax.dynamic_slice_in_dim(q, s0, QB, axis=3)

        sc = jnp.einsum('bghqd,bgnd->bghqn', qc, kc, preferred_element_type=jnp.float32) * scale
        cmask = cmp_end[None, :] <= tq[:, None]
        pc = jax.nn.softmax(jnp.where(cmask, sc, NEG), axis=-1) * cmask
        o_cmp = jnp.einsum('bghqn,bgnd->bghqd', pc.astype(vc.dtype), vc)

        imp = jnp.einsum('bghqn,nj->bgqj', pc, overlap)
        jq = s0 // SB
        forced = (blk_ids == 0) | (blk_ids == jq) | (blk_ids == jq - 1)
        imp = jnp.where(blk_ids > jq, NEG, jnp.where(forced, FORCE, imp))
        _, sel = lax.top_k(imp, top_n)
        kg = ks_blk[bi, gi, sel].reshape(B, G, QB, top_n * SB, dh)
        vg = vs_blk[bi, gi, sel].reshape(B, G, QB, top_n * SB, dh)
        kpos = (sel[..., None] * SB + jnp.arange(SB)).reshape(B, G, QB, top_n * SB)
        smask = (kpos <= tq[None, None, :, None])[:, :, None]
        ss = jnp.einsum('bghqd,bgqkd->bghqk', qc, kg, preferred_element_type=jnp.float32) * scale
        ps = jax.nn.softmax(jnp.where(smask, ss, NEG), axis=-1)
        o_slc = jnp.einsum('bghqk,bgqkd->bghqd', ps.astype(vg.dtype), vg)

        kwc = lax.dynamic_slice_in_dim(kw_pad, s0, W + QB, axis=2)
        vwc = lax.dynamic_slice_in_dim(vw_pad, s0, W + QB, axis=2)
        wpos = s0 - W + jnp.arange(W + QB)
        wmask = (wpos[None, :] <= tq[:, None]) & (wpos[None, :] > tq[:, None] - W) & (wpos[None, :] >= 0)
        sw = jnp.einsum('bghqd,bgkd->bghqk', qc, kwc, preferred_element_type=jnp.float32) * scale
        pw = jax.nn.softmax(jnp.where(wmask, sw, NEG), axis=-1)
        o_win = jnp.einsum('bghqk,bgkd->bghqd', pw.astype(vwc.dtype), vwc)
        return o_cmp, o_slc, o_win

    o_cmp, o_slc, o_win = lax.map(chunk, jnp.arange(S // QB))

    def heads(o):
        return _merge_chunks(o.reshape(-1, B, N_HEADS, QB, dh)).reshape(B, S, N_HEADS, dh)

    g = jax.nn.sigmoid(gates).reshape(B, S, 3, N_HEADS, 1)
    o = g[:, :, 0] * heads(o_cmp) + g[:, :, 1] * heads(o_slc) + g[:, :, 2] * heads(o_win)
    return o.reshape(B, S, D_MODEL) @ w_out

def moba_mixer(h, w_in, w_out):
    B, S, _ = h.shape
    BLK, QB, dh, H = MOBA_BLOCK, MOBA_QB, HEAD_DIM, N_HEADS
    nb = -(-S // BLK)
    s_pad = nb * BLK
    top_k = min(MOBA_TOPK, nb)
    n_g = top_k * BLK
    scale = dh ** -0.5

    q, k, v = jnp.split(h @ w_in, 3, axis=-1)
    cos, sin = rope_tables(jnp.arange(S))
    q = apply_rope(_split_heads(q, H), cos, sin)
    k = apply_rope(_split_heads(k, H), cos, sin)
    v = _split_heads(v, H)
    padw = ((0, 0), (0, 0), (0, s_pad - S), (0, 0))
    k_blk = jnp.pad(k, padw).reshape(B, H, nb, BLK, dh)
    v_blk = jnp.pad(v, padw).reshape(B, H, nb, BLK, dh)
    k_mean = k_blk.astype(jnp.float32).mean(axis=3)
    bi = jnp.arange(B)[:, None, None, None]
    hi = jnp.arange(H)[None, :, None, None]
    blk_ids = jnp.arange(nb)

    def chunk(c):
        s0 = c * QB
        tq = s0 + jnp.arange(QB)
        cb = s0 // BLK
        qc = lax.dynamic_slice_in_dim(q, s0, QB, axis=2)
        gsc = jnp.einsum('bhqd,bhnd->bhqn', qc.astype(jnp.float32), k_mean)
        gsc = jnp.where(blk_ids < cb, gsc, NEG)
        _, sel = lax.top_k(gsc, top_k)
        valid = jnp.repeat(sel < cb, BLK, axis=-1)
        kg = k_blk[bi, hi, sel].reshape(B, H, QB, n_g, dh)
        vg = v_blk[bi, hi, sel].reshape(B, H, QB, n_g, dh)
        ko = k_blk[:, :, cb]
        vo = v_blk[:, :, cb]
        omask = (cb * BLK + jnp.arange(BLK))[None, :] <= tq[:, None]
        sg = jnp.einsum('bhqd,bhqkd->bhqk', qc, kg, preferred_element_type=jnp.float32) * scale
        so = jnp.einsum('bhqd,bhkd->bhqk', qc, ko, preferred_element_type=jnp.float32) * scale
        s = jnp.concatenate([jnp.where(valid, sg, NEG), jnp.where(omask, so, NEG)], axis=-1)
        p = jax.nn.softmax(s, axis=-1).astype(v.dtype)
        return (jnp.einsum('bhqk,bhqkd->bhqd', p[..., :n_g], vg)
                + jnp.einsum('bhqk,bhkd->bhqd', p[..., n_g:], vo))

    o = lax.map(chunk, jnp.arange(S // QB))
    return _merge_chunks(o) @ w_out

def grouped_moe(h, router_w, router_bias, w_gate, w_up, w_down):
    B, S, D = h.shape
    xt = h.reshape(B * S, D)
    scores = jax.nn.sigmoid((xt @ router_w).astype(jnp.float32))
    biased = scores + router_bias.astype(jnp.float32)
    grp = biased.reshape(-1, N_GROUPS, EXPERTS_PER_GROUP)
    grp_score = lax.top_k(grp, 2)[0].sum(-1)
    _, g_sel = lax.top_k(grp_score, 1)
    emask = jnp.repeat(jnp.arange(N_GROUPS)[None, :] == g_sel, EXPERTS_PER_GROUP, axis=-1)
    _, e_sel = lax.top_k(jnp.where(emask, biased, NEG), TOP_K)
    w_sel = jnp.take_along_axis(scores, e_sel, axis=-1)
    w_sel = w_sel / w_sel.sum(-1, keepdims=True)
    gate = jnp.einsum('tk,tke->te', w_sel, jax.nn.one_hot(e_sel, N_EXPERTS, dtype=jnp.float32)).astype(xt.dtype)
    out = jnp.zeros_like(xt)
    for e in range(N_EXPERTS):
        he = jax.nn.silu(xt @ w_gate[e]) * (xt @ w_up[e])
        out = out + (he @ w_down[e]) * gate[:, e:e + 1]
    return out.reshape(B, S, D)

def setup_inputs(seed: int = 0) -> dict:
    key = jax.random.key(seed)
    ks = jax.random.split(key, 18)
    f32 = jnp.float32
    nrm = lambda k, shape, s: jax.random.normal(k, shape, f32) * s
    beta = DN_BETA
    KV = NSA_KV_DIM
    nsa_col = np.concatenate([np.ones(D_MODEL), np.ones(KV), np.full(KV, beta), np.ones(KV),
                              np.full(KV, beta), np.ones(KV), np.full(KV, beta),
                              np.ones(3 * N_HEADS)]).astype(np.float32)
    moba_col = np.concatenate([np.ones(2 * D_MODEL), np.full(D_MODEL, beta)]).astype(np.float32)
    cmp_in = NSA_CMP_LEN * HEAD_DIM
    return {
        'x': jax.random.normal(ks[0], (BATCH, SEQ, D_MODEL), f32),
        'nsa_w_in': nrm(ks[1], (N_NSA_LAYERS, D_MODEL, NSA_IN_DIM), D_MODEL ** -0.5) * jnp.asarray(nsa_col),
        'nsa_w_out': nrm(ks[2], (N_NSA_LAYERS, D_MODEL, D_MODEL), D_MODEL ** -0.5 * beta),
        'nsa_cmp_k_w1': nrm(ks[3], (N_NSA_LAYERS, cmp_in, NSA_CMP_HIDDEN), cmp_in ** -0.5),
        'nsa_cmp_k_w2': nrm(ks[4], (N_NSA_LAYERS, NSA_CMP_HIDDEN, HEAD_DIM), NSA_CMP_HIDDEN ** -0.5),
        'nsa_cmp_v_w1': nrm(ks[5], (N_NSA_LAYERS, cmp_in, NSA_CMP_HIDDEN), cmp_in ** -0.5),
        'nsa_cmp_v_w2': nrm(ks[6], (N_NSA_LAYERS, NSA_CMP_HIDDEN, HEAD_DIM), NSA_CMP_HIDDEN ** -0.5 * beta),
        'nsa_cmp_k_pos': nrm(ks[7], (N_NSA_LAYERS, NSA_CMP_LEN, HEAD_DIM), 0.1),
        'nsa_cmp_v_pos': nrm(ks[8], (N_NSA_LAYERS, NSA_CMP_LEN, HEAD_DIM), 0.1),
        'moba_w_in': nrm(ks[9], (N_MOBA_LAYERS, D_MODEL, MOBA_IN_DIM), D_MODEL ** -0.5) * jnp.asarray(moba_col),
        'moba_w_out': nrm(ks[10], (N_MOBA_LAYERS, D_MODEL, D_MODEL), D_MODEL ** -0.5 * beta),
        'router_w': nrm(ks[11], (D_MODEL, N_EXPERTS), D_MODEL ** -0.5),
        'router_bias': nrm(ks[12], (N_EXPERTS,), 0.01),
        'moe_w_gate': nrm(ks[13], (DEPTH, N_EXPERTS, D_MODEL, D_EXPERT), D_MODEL ** -0.5),
        'moe_w_up': nrm(ks[14], (DEPTH, N_EXPERTS, D_MODEL, D_EXPERT), D_MODEL ** -0.5),
        'moe_w_down': nrm(ks[15], (DEPTH, N_EXPERTS, D_EXPERT, D_MODEL), D_EXPERT ** -0.5 * beta),
        'ln_g': 1.0 + nrm(ks[16], (DEPTH, 2, D_MODEL), 0.05),
        'ln_b': nrm(ks[17], (DEPTH, 2, D_MODEL), 0.05),
    }

def reference(x, nsa_w_in, nsa_w_out, nsa_cmp_k_w1, nsa_cmp_k_w2, nsa_cmp_v_w1, nsa_cmp_v_w2,
              nsa_cmp_k_pos, nsa_cmp_v_pos, moba_w_in, moba_w_out, router_w, router_bias,
              moe_w_gate, moe_w_up, moe_w_down, ln_g, ln_b):
    for layer in range(DEPTH):
        j = layer // N_MIXERS
        if layer % N_MIXERS == 0:
            mix = nsa_mixer(x, nsa_w_in[j], nsa_w_out[j], nsa_cmp_k_w1[j], nsa_cmp_k_w2[j],
                            nsa_cmp_v_w1[j], nsa_cmp_v_w2[j], nsa_cmp_k_pos[j], nsa_cmp_v_pos[j])
        else:
            mix = moba_mixer(x, moba_w_in[j], moba_w_out[j])
        x = layer_norm(DN_ALPHA * x + mix, ln_g[layer, 0], ln_b[layer, 0])
        ffn = grouped_moe(x, router_w, router_bias, moe_w_gate[layer], moe_w_up[layer], moe_w_down[layer])
        x = layer_norm(DN_ALPHA * x + ffn, ln_g[layer, 1], ln_b[layer, 1])
    return x


_drawn_inputs = setup_inputs


def setup_inputs(seed=0):
    import zlib

    import numpy as np

    out = dict(_drawn_inputs(seed))
    spreads = {}
    factors = {'nsa_cmp_k_w1': 3.705, 'nsa_cmp_k_w2': 3.61, 'nsa_cmp_k_pos': 8.0, 'nsa_cmp_v_pos': 3.051}
    for name, (base, spread) in spreads.items():
        noise = np.random.default_rng([zlib.crc32(name.encode()), seed]).standard_normal(out[name].shape)
        drawn = base * np.exp(spread * noise) if base else spread * noise
        out[name] = __import__('jax').numpy.asarray(drawn.astype(out[name].dtype))
    for name, factor in factors.items():
        out[name] = (out[name] * factor).astype(out[name].dtype)
    return out
```

```python
from collections import namedtuple
from contextlib import ExitStack

import numpy as np
import concourse.bass as bass
from concourse import mybir

F32 = mybir.dt.float32
BF16 = mybir.dt.bfloat16
I32 = mybir.dt.int32
ALU = mybir.AluOpType
ACT = mybir.ActivationFunctionType
AX = mybir.AxisListType

P = 128
D, S = 1024, 256
T = S // P
KJ = D // P
H, DH = 16, 64
G, HPG = 4, 4
UNIT = 512
NEG = -1e30
ALPHA = 4.0 ** 0.25
EPS = 1e-5
CL, CS = 32, 16
NC = (S - CL) // CS + 1
CH = 256
E, EG = 16, 4
FE = 512
FJ = FE // P
PAIRS = E // 2
SLOTS = 64
ROUNDS = S // SLOTS
RING = 6

CONST = {}
_at = 0
for _name, _n in (("ident", P), ("alphai", P), ("causal", P), ("before", P), ("ones", P),
                  ("cosq", T * DH), ("sinq", T * DH), ("cosk", T * DH), ("sink", T * DH),
                  ("cmask", T * G * DH), ("ccos", DH), ("csin", DH), ("slot", SLOTS), ("lower", EG * EG)):
    CONST[_name] = (_at, _n)
    _at += _n
NCONST = _at


def constants():
    c = np.zeros((P, NCONST), np.float32)

    def put(name, a):
        at, n = CONST[name]
        c[:a.shape[0], at:at + n] = a.reshape(a.shape[0], n)

    p = np.arange(P)
    put("ident", np.eye(P))
    put("alphai", np.eye(P) * ALPHA)
    put("causal", np.where(p[None, :] > p[:, None], NEG, 0.0))
    put("before", (p[:, None] < p[None, :]) * 1.0)
    put("ones", np.ones((P, P)))
    f = np.float32
    inv = f(1.0) / (f(10000.0) ** (np.arange(0, DH, 2, dtype=f) / f(DH)))

    def rope(pos):
        ang = pos.astype(f)[:, None] * inv[None, :]
        cos, sin = np.cos(ang), np.sin(ang)
        return np.concatenate([cos, cos], 1), np.concatenate([-sin, sin], 1)

    cos, sin = rope(np.arange(S))
    tiles = lambda a: a.reshape(T, P, -1).transpose(1, 0, 2)
    put("cosk", tiles(cos))
    put("sink", tiles(sin))
    put("cosq", tiles(cos * f(DH ** -0.5)))
    put("sinq", tiles(sin * f(DH ** -0.5)))
    end = np.arange(NC) * CS + CL - 1
    cos, sin = rope(end)
    put("ccos", np.tile(cos, (G, 1)))
    put("csin", np.tile(sin, (G, 1)))
    m = np.full((S, G, DH), NEG, f)
    for g in range(G):
        m[:, g, g * NC:(g + 1) * NC] = np.where(end[None, :] <= np.arange(S)[:, None], 0.0, NEG)
    put("cmask", tiles(m.reshape(S, G * DH)))
    put("slot", np.broadcast_to(np.arange(SLOTS), (P, SLOTS)))
    put("lower", np.broadcast_to((np.arange(EG)[None, :] < np.arange(EG)[:, None]) * 1.0, (P, EG, EG)))
    return c


def build(nc, x, consts, w_in0, w_out0, cmp_kw1, cmp_kw2, cmp_vw1, cmp_vw2, cmp_kpos, cmp_vpos,
          w_in1, w_out1, router_w, router_b, w_gate, w_up, w_down, ln_g, ln_b, out):
    ctx = ExitStack()
    with ctx:
        def sb(name, shape, dt=F32):
            return ctx.enter_context(nc.sbuf_tensor(name, shape, dt))

        def sem(name):
            return ctx.enter_context(nc.semaphore(name))

        ring = sb("ring", [P, RING, KJ * UNIT])
        area = sb("area", [P, 2, KJ, UNIT])
        cst = sb("cst", [P, NCONST])
        X = sb("X", [P, T, D])
        R1 = sb("R1", [P, T * D])
        R2 = sb("R2", [P, T * D])
        R3 = sb("R3", [P, T * D])
        R4 = sb("R4", [P, T * D])
        R5 = sb("R5", [P, 3 * D])
        R6 = sb("R6", [P, 3 * D])
        small = sb("small", [P, 1024])
        wgt = sb("wgt", [P, KJ, 3 * H])
        rw = sb("rw", [P, KJ, E])
        identb = sb("identb", [P, P], BF16)
        causalb = sb("causalb", [P, P], BF16)
        over = sb("over", [1, 2], I32)
        ps = ctx.enter_context(nc.psum_tensor("ps", [P, 8, 512], F32))

        def const(name):
            at, n = CONST[name]
            return cst[:, at:at + n]

        ident = const("ident")
        used = [0]

        def tiny(n):
            used[0] += n
            assert used[0] <= 1024
            return small[:, used[0] - n:used[0]]

        xT = R1[:, :].rearrange("p (j t) -> p j t", j=KJ)
        O = R1[:, :].rearrange("p (a c) -> p a c", a=T)
        qT = R2[:, :].rearrange("p (j t) -> p j t", j=KJ)
        OT = qT
        Xp = R2[:, :].rearrange("p (a j c) -> p a j c", a=T, j=KJ)
        XeT = R3[:, 0:KJ * P].rearrange("p (j c) -> p j c", j=KJ)
        Y = R3[:, D:2 * D]
        stage = [R6[:, n * UNIT:(n + 1) * UNIT] for n in range(2)]
        rope_b = [R6[:, (2 + n) * UNIT:(3 + n) * UNIT] for n in range(2)]
        Pb = [R5[:, n * 768:(n + 1) * 768].rearrange("p (a k) -> p a k", a=2) for n in range(2)]
        PTb = [R5[:, 1536 + n * 768:1536 + (n + 1) * 768].rearrange("p (a k) -> p a k", a=2) for n in range(2)]
        otmp = [R6[:, n * UNIT:(n + 1) * UNIT] for n in range(2)]
        Sc = R6[:, D:3 * D].rearrange("p (a h k) -> p a h k", a=T, h=H)
        lnw = R5[:, 0:2 * D].rearrange("p (w c) -> p w c", w=2)
        stat_kv = [R5[:, n * 960:(n + 1) * 960].rearrange("p (m g n) -> p m g n", m=CL // 2, g=G) for n in range(2)]
        raw = R2[:, :].rearrange("p (a g u c) -> p a g u c", a=T, g=2 * G, u=2)
        PTc = R5[:, 0:2 * D].rearrange("p (a j t) -> p a j t", a=T, j=H // 2)
        hg = R4[:, D:D + CH]
        hgT = R4[:, D + 256:D + 512].rearrange("p (k c) -> p k c", k=2)
        w2 = R4[:, D + 512:D + 768].rearrange("p (w k c) -> p w k c", w=2, k=2)
        kcT = R4[:, D + 768:D + 832]
        vcb = R4[:, D + 832:D + 960]
        kca = R3[:, D:D + 64]
        kcb = R3[:, D + 64:D + 128]
        kcr = R3[:, D + 128:D + 256]
        hid = R4[:, 0:FE]
        sg = R4[:, FE:2 * FE]
        hT = R4[:, 2 * FE:3 * FE].rearrange("p (k c) -> p k c", k=FJ)
        Pm = R4[:, 1536:1792].rearrange("p (a e c) -> p a e c", a=T, e=2)
        GP = R4[:, 1792:2048].rearrange("p (a e c) -> p a e c", a=T, e=2)
        GT = R6[:, 0:256].rearrange("p (a c) -> p a c", a=T)

        gates = tiny(T * 3 * H).rearrange("p (a h) -> p a h", a=T)
        posT = tiny(2 * 16).rearrange("p (w m) -> p w m", w=2)
        sums = tiny(16 * 8).rearrange("p (q a r h) -> p q a r h", q=16, a=T, r=2)
        nmax = tiny(8).rearrange("p (b a h) -> p b a h", b=2, a=T)
        coef = tiny(16).rearrange("p (b a r h) -> p b a r h", b=2, a=T, r=2)
        cmax = tiny(T * H).rearrange("p (a h) -> p a h", a=T)
        csum = tiny(T * H).rearrange("p (a h) -> p a h", a=T)
        bst = tiny(T * 12).rearrange("p (a h s) -> p a h s", a=T, h=2)
        mv = tiny(T * 2).rearrange("p (a s) -> p a s", a=T)
        ve = tiny(T)
        half = tiny(T)
        rstd = tiny(T)
        rb = tiny(E)
        sc = tiny(T * E).rearrange("p (a e) -> p a e", a=T)
        bs = tiny(T * E).rearrange("p (a e) -> p a e", a=T)
        cg = tiny(T * E * EG)
        ch = tiny(T * E * EG)
        rank = tiny(T * E)
        sel2 = tiny(T * E)
        gs = tiny(T * EG)
        gsel = tiny(T * EG)
        sel = tiny(T * E).rearrange("p (a e) -> p a e", a=T)
        wsum = tiny(T)
        EP = E + 2
        pos = tiny(T * EP).rearrange("p (a e) -> p a e", a=T)
        gate = tiny(T * EP).rearrange("p (a e) -> p a e", a=T)

        x_in, c_in, s_in = sem("x_in"), sem("c_in"), sem("s_in")
        cmpw_in = sem("cmpw_in")
        area_in = [sem("area_in0"), sem("area_in1")]
        cmpw_used = sem("cmpw_used")
        bconst = sem("bconst")
        out_done = sem("out_done")
        padded, round_over = sem("padded"), sem("round_over")
        o_mul, cs_max = sem("o_mul"), sem("cs_max")
        dve_step, pool_step = sem("dve_step"), sem("pool_step")
        LS = namedtuple("LS", "xt xt_sb proj rope_mul roped copied tr tr_copied s_done mx exp pt pt_sb pv o_ev "
                              "o_half o_add o_t ot_sb mix ln_in")
        L = LS(*(sem(n) for n in LS._fields))
        base = [LS(*[0] * len(LS._fields)),
                LS(xt=4, xt_sb=4, proj=11, rope_mul=8, roped=8, copied=7, tr=8, tr_copied=8, s_done=16, mx=32, exp=16,
                   pt=16, pt_sb=32, pv=16, o_ev=8, o_half=8, o_add=12, o_t=4, ot_sb=4, mix=4, ln_in=32)]
        kcvc_t, stat_done, h_done, gelu, hg_t, hgt_sb, w2_done, kc_rope, kc_add, vc_done, kct, kct_sb, hg_zero = (
            sem(n) for n in "kcvc_t stat_done h_done gelu hg_t hgt_sb w2_done kc_rope kc_add vc_done kct kct_sb hg_zero".split())
        cs_done, cs_masked, cs_sub, cs_exp, cs_p, cp_t, cp_sb, cp_sb2, cpv = (
            sem(n) for n in "cs_done cs_masked cs_sub cs_exp cs_p cp_t cp_sb cp_sb2 cpv".split())
        LN = namedtuple("LN", "stats rstd scaled x_ready")
        N = LN(*(sem(f"ln_{n}") for n in LN._fields))
        RT = namedtuple("RT", "xt xt_sb logits score sel pos table over xp ln_in")
        R = RT(*(sem(f"route_{n}") for n in RT._fields))
        rbase = [RT(*[0] * len(RT._fields)), RT(4, 4, 1, 1, 1, 1, 1, 1, T, 32)]
        RD = namedtuple("RD", "w gate_done up_done gathered onehot gp silu h xe gt gt_copied ht ht_sb "
                              "y y_d y_a comb shift")
        rounds = [RD([sem(f"w{s}_{k}") for s in range(3)], *(sem(f"{n}_{k}") for n in RD._fields[1:]))
                  for k in ("main", "more0", "more1")]
        main = rounds[0]

        NSA_COLS = [1024, 1536, 2048, 0, 512]
        ROPE0 = [2, 0]
        ROPED = [8, 8]
        LAST = [11, 12]
        AREA0 = [0, 7]
        OUT0 = [5, 13]

        def ropes(l, n):
            return max(0, min(n + 1 - ROPE0[l], ROPED[l]))

        def copies(l, n):
            return min(n + 1, 6) + (n >= 10) if l == 0 else max(0, n + 1 - 8)

        block = ctx.enter_context(nc.Block())

        @block.sync
        def _(sp):
            def unit_src(u):
                if u < 5:
                    return w_in0[:, NSA_COLS[u]:NSA_COLS[u] + UNIT]
                if u < 7:
                    return w_out0[:, (u - 5) * UNIT:(u - 4) * UNIT]
                if u < 13:
                    return w_in1[:, (u - 7) * UNIT:(u - 6) * UNIT]
                return w_out1[:, (u - 13) * UNIT:(u - 12) * UNIT]

            def load_unit(u):
                if 2 <= u < 7:
                    sp.wait_ge(L.proj, 2 * (u - 1))
                elif 7 <= u < 9:
                    sp.wait_ge(L.mix, 2 * (u - 6))
                elif u >= 9:
                    sp.wait_ge(L.proj, base[1].proj + 2 * (u - 8))
                sp.dma_start(area[:, u % 2], unit_src(u).rearrange("(j p) n -> p j n", p=P)).then_inc(area_in[u % 2], 16)

            def load_slot(rd, l, i, s):
                w = (w_gate, w_up, w_down)[s // 2]
                src = w[l, bass.ds(i, 1)] if not isinstance(i, int) else w[l, i:i + 1]
                if s < 4:
                    sp.dma_start(ring[:, s], src.rearrange("a (p j) n -> p (a j n)", p=P)).then_inc(rd.w[s // 2], 16)
                else:
                    sp.dma_start(ring[:, s].rearrange("p (k n) -> p k n", k=FJ),
                                 src.rearrange("a (k p) n -> p (a k) n", p=P)).then_inc(rd.w[s // 2], 16)

            def load_ln(k, signal):
                l, s = k // 2, k % 2
                sp.dma_start(lnw[:, 0], ln_g[l, s:s + 1].to_broadcast([P, D])).then_inc(signal, 16)
                sp.dma_start(lnw[:, 1], ln_b[l, s:s + 1].to_broadcast([P, D])).then_inc(signal, 16)

            def rest_of_round(rd, l, rho):
                with sp.Fori(1, PAIRS) as i:
                    n, n2 = sp.snap(i + PAIRS * rho), sp.snap(2 * i + 2 * PAIRS * rho)
                    experts = [sp.snap(2 * i), sp.snap(2 * i + 1)]
                    for s in range(RING):
                        if s < 2:
                            sp.wait_ge(rd.gate_done, n)
                        elif s < 4:
                            sp.wait_ge(rd.up_done, n)
                        else:
                            sp.wait_ge(rd.y, n2)
                        load_slot(rd, l, experts[s % 2], s)

            sp.dma_start(X[:, :, :], x.rearrange("(a p) c -> p a c", p=P)).then_inc(x_in, 16)
            sp.dma_start(cst[:, :], consts).then_inc(c_in, 16)
            load_unit(0)
            load_unit(1)
            for s, (w2_, pos_) in enumerate(((cmp_kw2, cmp_kpos), (cmp_vw2, cmp_vpos))):
                sp.dma_start(w2[:, s], w2_.rearrange("(k p) n -> p k n", p=P)).then_inc(s_in, 16)
                sp.dma_start(posT[:, s], pos_).then_inc(s_in, 16)
            sp.dma_start(wgt[:, :, :], w_in0[:, 2560:2608].rearrange("(j p) n -> p j n", p=P)).then_inc(s_in, 16)
            sp.dma_start(rw[:, :, :], router_w.rearrange("(j p) n -> p j n", p=P)).then_inc(s_in, 16)
            sp.dma_start(rb, router_b.to_broadcast([P, E])).then_inc(s_in, 16)
            for s, w in ((4, cmp_kw1), (5, cmp_vw1)):
                sp.dma_start(ring[:, s].rearrange("p (m n) -> p m n", m=CL // 2),
                             w.rearrange("(m p) n -> p m n", p=P)).then_inc(cmpw_in, 16)
            load_slot(main, 0, 0, 0)
            load_unit(2)
            load_slot(main, 0, 1, 1)
            load_unit(3)
            load_slot(main, 0, 0, 2)
            load_unit(4)
            load_slot(main, 0, 1, 3)
            sp.wait_ge(cmpw_used, 1)
            load_slot(main, 0, 0, 4)
            load_slot(main, 0, 1, 5)
            load_unit(5)
            load_unit(6)
            for l in range(2):
                B, C, extra = base[l], rbase[l], rounds[1 + l]
                if l == 0:
                    sp.wait_ge(cpv, 2)
                else:
                    sp.wait_ge(L.pv, B.pv + 8)
                load_ln(2 * l, L.ln_in)
                if l == 0:
                    load_unit(7)
                    load_unit(8)
                sp.wait_ge(N.x_ready, 2 * l * T + T)
                load_ln(2 * l + 1, R.ln_in)
                rest_of_round(main, l, l)
                sp.wait_ge(R.over, C.over + 1)
                most = sp.value_load(over[0:1, 0:1], min_val=0, max_val=S)
                with sp.If(most > SLOTS):
                    sp.wait_ge(main.comb, PAIRS * (l + 1))
                    with sp.Fori(0, ROUNDS - 1) as rho:
                        for s in range(RING):
                            load_slot(extra, l, s % 2, s)
                        rest_of_round(extra, l, rho)
                        sp.wait_ge(extra.comb, PAIRS * rho + PAIRS)
                        sp.sem_inc(round_over, 1)
                if l == 0:
                    for s in range(RING):
                        sp.wait_ge(main.gate_done if s < 2 else main.up_done if s < 4 else main.y,
                                   PAIRS if s < 4 else 2 * PAIRS)
                        load_slot(main, 1, s % 2, s)
                    for u in range(9, 15):
                        load_unit(u)
            for a in range(T):
                sp.wait_ge(N.x_ready, 3 * T + a + 1)
                sp.dma_start(out[a * P:(a + 1) * P, :], X[:, a]).then_inc(out_done, 16)
            sp.wait_ge(out_done, 16 * T)

        def bc(ap, axis, n):
            ap = ap.unsqueeze(axis)
            shape = list(ap.shape)
            shape[axis] = n
            return ap.to_broadcast(shape)

        ITEMS = [[(4 * gp + i, 2 * br + gp, [256 * br + 64 * (2 * gp + a) for a in range(2)])
                  for br in range(2) for gp in range(2) for i in range(HPG)],
                 [(j, j, [128 * j + 64 * a for a in range(2)]) for j in range(H // 2)]]
        V = [R4[:, 0:D].rearrange("p (a c) -> p a c", a=T), R4[:, :].rearrange("p (a c) -> p a c", a=T)]
        kT = R3[:, :].rearrange("p (j t) -> p j t", t=S)
        AREA_IN = lambda u: (area_in[u % 2], 16 * (u // 2 + 1))

        def heads(l, q):
            if l:
                return 4 * q, 2, 1
            return 8 * (q % 4 // 2) + 2 * (q % 2), 1, 4

        @block.tensor
        def _(pe):
            mm, tp = nc.tensor.matmul, nc.tensor.transpose

            def transpose_tokens(src, signal, ready):
                for a in range(T):
                    ready(a)
                    for m in range(4):
                        for jj in range(2):
                            j = 2 * m + jj
                            last = tp(ps[:, m, jj * S + a * P:jj * S + (a + 1) * P], src[:, a, j * P:(j + 1) * P], ident)
                        if a == T - 1:
                            last.then_inc(signal, 1)

            def project(l, n):
                B = base[l]
                u = AREA0[l] + n // 2
                if n % 2 == 0:
                    pe.wait_ge(*AREA_IN(u))
                if n >= 4:
                    if ropes(l, n - 4):
                        pe.wait_ge(L.rope_mul, B.rope_mul + ropes(l, n - 4))
                    if copies(l, n - 4):
                        pe.wait_ge(L.copied, B.copied + copies(l, n - 4))
                a = n % 2
                for j in range(KJ):
                    last = mm(ps[:, n % 4, :], xT[:, j, a * P:(a + 1) * P], area[:, u % 2, j, :],
                              start=(j == 0), stop=(j == KJ - 1))
                last.then_inc(L.proj, 1)

            def transpose_roped(l, r):
                B = base[l]
                pe.wait_ge(L.roped, B.roped + r + 1)
                if r >= 2:
                    pe.wait_ge(L.tr_copied, B.tr_copied + r - 1)
                elif l == 0:
                    pe.wait_ge(stat_done, 8)
                narrow = l == 0 and r < 4
                for b in range(2 if narrow else 4):
                    st = stage[r % 2]
                    last = tp(ps[:, 4 + r % 2, b * P:(b + 1) * P], st[:, b * P:(b + 1) * P], ident)
                last.then_inc(L.tr, 1)

            def scores(l, m):
                B = base[l]
                jq, jk, _ = ITEMS[l][m]
                if m == 0:
                    pe.wait_ge(L.tr_copied, B.tr_copied + 8)
                    pe.wait_ge(L.copied, B.copied + copies(l, LAST[l] - 1))
                    pe.wait_ge(bconst, 2)
                if m >= 2:
                    pe.wait_ge(L.exp, B.exp + m - 1)
                for t in range(T):
                    at, n = t * P, (t + 1) * P
                    for a in range(2):
                        h = slice(64 * a, 64 * a + 64)
                        mm(ps[:, 2 * (m % 2) + a, at:at + n], qT[h, jq, t * P:(t + 1) * P], kT[h, jk, 0:n],
                           start=True, stop=False)
                    for a in range(2):
                        last = mm(ps[:, 2 * (m % 2) + a, at + t * P:at + n], identb[:, :], causalb[:, :],
                                  start=False, stop=True)
                last.then_inc(L.s_done, 1)

            def transpose_probs(l, m):
                B = base[l]
                pe.wait_ge(L.exp, B.exp + m + 1)
                if m >= 1:
                    pe.wait_ge(L.pt_sb, B.pt_sb + 2 * m)
                for a in range(2):
                    for b in range(3):
                        last = tp(ps[:, 4 + a, b * P:(b + 1) * P], Pb[m % 2][:, a, b * P:(b + 1) * P], ident)
                last.then_inc(L.pt, 1)

            def times_v(l, m):
                B = base[l]
                q = m // 2
                pe.wait_ge(L.pt_sb, B.pt_sb + 2 * m + 2)
                if q >= 2:
                    pe.wait_ge(L.o_ev, B.o_ev + q - 1)
                elif q == 0 and l == 0:
                    pe.wait_ge(kct_sb, 1)
                    pe.wait_ge(vc_done, 1)
                    pe.wait_ge(kc_rope, 1)
                o = ps[:, 6 + q % 2, :].rearrange("p (t r a c) -> p t r a c", t=T, r=2, a=2)
                for a in range(2):
                    c = ITEMS[l][m][2][a]
                    pt = PTb[m % 2]
                    mm(o[:, 0, m % 2, a, :], pt[:, a, 0:P], V[l][:, 0, c:c + DH], start=True, stop=True)
                    mm(o[:, 1, m % 2, a, :], pt[:, a, P:2 * P], V[l][:, 0, c:c + DH], start=True, stop=False)
                    last = mm(o[:, 1, m % 2, a, :], pt[:, a, 2 * P:3 * P], V[l][:, 1, c:c + DH], start=False, stop=True)
                last.then_inc(L.pv, 1)

            def compressed_scores(t):
                if t == 0:
                    pe.wait_ge(L.exp, 15)
                    pe.wait_ge(kct_sb, 1)
                else:
                    pe.wait_ge(L.exp, 16)
                for i in range(H // 2):
                    for a in range(2):
                        r = slice(64 * a, 64 * a + 64)
                        last = mm(ps[:, 2 * t + a, i * DH:(i + 1) * DH], qT[r, i, t * P:(t + 1) * P],
                                  kcT[r, :], start=True, stop=True)
                last.then_inc(cs_done, 1)

            def attention(l):
                n = len(ITEMS[l])
                for m in range(n):
                    scores(l, m)
                    if m >= 1:
                        transpose_probs(l, m - 1)
                    if m >= 2:
                        times_v(l, m - 2)
                if l == 0:
                    compressed_scores(0)
                transpose_probs(l, n - 1)
                times_v(l, n - 2)
                if l == 0:
                    compressed_scores(1)
                times_v(l, n - 1)
                if l == 0:
                    for t in range(T):
                        pe.wait_ge(cs_p, t + 1)
                        if t == 0:
                            pe.wait_ge(L.pt_sb, B.pt_sb + 32)
                        b = 4 if t == 0 else 0
                        for j in range(H // 2):
                            last = tp(ps[:, b + j // 4, (j % 4) * P:(j % 4 + 1) * P],
                                      Sc[:, t, 2 * j:2 * j + 2, :].rearrange("p h k -> p (h k)"), ident)
                        last.then_inc(cp_t, 1)
                    for t in range(T):
                        pe.wait_ge(cp_sb, t + 1)
                        pe.wait_ge(cp_sb2, t + 1)
                        if t == 0:
                            pe.wait_ge(L.o_ev, 8)
                        b = 6 if t == 0 else 2
                        for j in range(H // 2):
                            a, gp, i = j // 4, j // 2 % 2, j % 2
                            last = mm(ps[:, b + gp, (2 * a + i) * P:(2 * a + i + 1) * P], PTc[:, t, j, :], vcb,
                                      start=True, stop=True)
                        last.then_inc(cpv, 1)

            def mix_out(l):
                B = base[l]
                def ready(a):
                    if l == 0:
                        pe.wait_ge(o_mul, 4)
                        pe.wait_ge(L.o_add, 8 + 2 * a + 2)
                    else:
                        pe.wait_ge(L.o_ev if a else L.o_half, (B.o_ev if a else B.o_half) + 4)
                transpose_tokens(O, L.o_t, ready)
                for a in range(T):
                    for w in range(2):
                        mm(ps[:, 4 + 2 * a + w, :], const("alphai"), X[:, a, w * UNIT:(w + 1) * UNIT],
                           start=True, stop=False, skip_group_check=True)
                pe.wait_ge(L.ot_sb, B.ot_sb + 4)
                for w in range(2):
                    u = OUT0[l] + w
                    pe.wait_ge(*AREA_IN(u))
                    for a in range(T):
                        for j in range(KJ):
                            last = mm(ps[:, 4 + 2 * a + w, :], OT[:, j, a * P:(a + 1) * P], area[:, u % 2, j, :],
                                      start=False, stop=(j == KJ - 1), skip_group_check=True)
                        last.then_inc(L.mix, 1)

            def gather(rd):
                for j in range(KJ):
                    for a in range(T):
                        last = mm(ps[:, 2 + j // 4, (j % 4) * P:(j % 4 + 1) * P], Xp[:, a, j, :],
                                  Pm[:, a].rearrange("p e c -> p (e c)"), start=(a == 0), stop=(a == T - 1))
                last.then_inc(rd.gathered, 1)

            def round_(rd, rho):
                pe.wait_ge(rd.onehot, (PAIRS + 1) * rho + 1)
                gather(rd)
                with pe.Fori(0, PAIRS) as i:
                    n, g = PAIRS * rho + i, (PAIRS + 1) * rho + i
                    pe.wait_ge(rd.xe, 2 * g + 2)
                    for w, done in ((0, rd.gate_done), (1, rd.up_done)):
                        pe.wait_ge(rd.w[w], 32 * n + 32)
                        for j in range(KJ):
                            for e in range(2):
                                last = mm(ps[64 * e:64 * e + 64, w, :], XeT[:, j, 64 * e:64 * e + 64],
                                          ring[:, 2 * w + e, j * UNIT:(j + 1) * UNIT], start=(j == 0), stop=(j == KJ - 1))
                        last.then_inc(done, 1)
                    pe.wait_ge(rd.onehot, g + 2)
                    gather(rd)
                    pe.wait_ge(rd.gp, g + 1)
                    pe.wait_ge(rd.h, n + 1)
                    for a in range(T):
                        last = tp(ps[:, 1, a * P:(a + 1) * P], GP[:, a].rearrange("p e c -> p (e c)"), ident)
                    last.then_inc(rd.gt, 1)
                    for k in range(FJ):
                        last = tp(ps[:, 0, k * P:(k + 1) * P], hid[:, k * P:(k + 1) * P], ident)
                    last.then_inc(rd.ht, 1)
                    pe.wait_ge(rd.xe, 2 * g + 4)
                    pe.wait_ge(rd.ht_sb, n + 1)
                    pe.wait_ge(rd.w[2], 32 * n + 32)
                    for w in range(2):
                        for k in range(FJ):
                            for e in range(2):
                                last = mm(ps[64 * e:64 * e + 64, 2 + w, :], hT[:, k, 64 * e:64 * e + 64],
                                          ring[:, 4 + e, k * D + w * UNIT:k * D + (w + 1) * UNIT],
                                          start=(k == 0), stop=(k == FJ - 1))
                        last.then_inc(rd.y, 1)
                    pe.wait_ge(rd.gt_copied, n + 1)
                    for w, copied in ((0, rd.y_d), (1, rd.y_a)):
                        pe.wait_ge(copied, n + 1)
                        for a in range(T):
                            last = mm(ps[:, 4 + 2 * a + w, :], GT[:, a, :], Y[:, w * UNIT:(w + 1) * UNIT],
                                      start=False, stop=True, skip_group_check=True)
                    last.then_inc(rd.comb, 1)

            pe.wait_ge(c_in, 16)
            for l in range(2):
                B, C = base[l], rbase[l]
                transpose_tokens(X, L.xt, (lambda a: pe.wait_ge(x_in, 16)) if l == 0 else
                                 (lambda a: pe.wait_ge(N.x_ready, T + a + 1)))
                pe.wait_ge(L.xt_sb, B.xt_sb + 4)
                if l == 0:
                    for n in range(4):
                        project(0, n)
                    pe.wait_ge(L.copied, B.copied + 2)
                    for w in range(2):
                        for g in range(G):
                            for a in range(T):
                                blk = raw[:, a, G * w + g].rearrange("p u c -> p (u c)")
                                last = tp(ps[:, 4 + 2 * w + g // 2, (g % 2) * S + a * P:(g % 2) * S + (a + 1) * P], blk, ident)
                            if g % 2:
                                last.then_inc(kcvc_t, 1)
                    project(0, 4)
                    project(0, 5)
                    transpose_roped(0, 0)
                    transpose_roped(0, 1)
                    pe.wait_ge(cmpw_in, 32)
                    pe.wait_ge(stat_done, 8)
                    for m in range(CL // 2):
                        for w in range(2):
                            last = mm(ps[64 * w:64 * w + G * NC, 6, 0:CH], stat_kv[w][:, m].rearrange("p g n -> p (g n)"),
                                      ring[:, 4 + w, m * CH:(m + 1) * CH], start=(m == 0), stop=(m == CL // 2 - 1))
                    last.then_inc(cmpw_used, 1)
                    project(0, 6)
                    project(0, 7)
                    transpose_roped(0, 2)
                    transpose_roped(0, 3)
                    pe.wait_ge(gelu, 2)
                    for k in range(2):
                        last = tp(ps[:, 7, k * P:(k + 1) * P], hg[:, k * P:(k + 1) * P], ident)
                    last.then_inc(hg_t, 1)
                    project(0, 8)
                    project(0, 9)
                    pe.wait_ge(hgt_sb, 1)
                    pe.wait_ge(s_in, 112)
                    for w in range(2):
                        for k in range(2):
                            last = mm(ps[0:G * NC, 6, w * DH:(w + 1) * DH], hgT[:, k, 64 * w:64 * w + G * NC],
                                      w2[:, w, k, :], start=(k == 0), stop=(k == 1))
                    last.then_inc(w2_done, 1)
                    transpose_roped(0, 4)
                    transpose_roped(0, 5)
                    pe.wait_ge(L.rope_mul, B.rope_mul + ropes(0, 6))
                    for a in range(T):
                        for j in range(KJ):
                            last = mm(ps[:, 10 % 4, a * 64:a * 64 + 3 * H], xT[:, j, a * P:(a + 1) * P], wgt[:, j, :],
                                      start=(j == 0), stop=(j == KJ - 1))
                    last.then_inc(L.proj, 1)
                    pe.wait_ge(kc_add, 1)
                    tp(ps[:, 7, 256:256 + G * NC], kcr[0:G * NC, :], ident[0:G * NC, 0:G * NC]).then_inc(kct, 1)
                    transpose_roped(0, 6)
                    transpose_roped(0, 7)
                else:
                    for n in range(4):
                        project(1, n)
                    for r in range(0, 8, 2):
                        transpose_roped(1, r)
                        transpose_roped(1, r + 1)
                        project(1, r + 4)
                        project(1, r + 5)
                attention(l)
                mix_out(l)
                transpose_tokens(X, R.xt, lambda a: pe.wait_ge(N.x_ready, 2 * l * T + a + 1))
                pe.wait_ge(R.xt_sb, C.xt_sb + 4)
                for a in range(T):
                    for j in range(KJ):
                        last = mm(ps[:, 0, a * E:(a + 1) * E], xT[:, j, a * P:(a + 1) * P], rw[:, j, :],
                                  start=(j == 0), stop=(j == KJ - 1))
                last.then_inc(R.logits, 1)
                for a in range(T):
                    for w in range(2):
                        mm(ps[:, 4 + 2 * a + w, :], const("alphai"), X[:, a, w * UNIT:(w + 1) * UNIT],
                           start=True, stop=True, skip_group_check=True)
                pe.wait_ge(R.sel, C.sel + 1)
                before, ones = const("before"), const("ones")
                mm(ps[:, 1, 0:E], before, sel[:, 0], start=True, stop=True)
                mm(ps[:, 1, E:2 * E], ones, sel[:, 0], start=True, stop=False)
                mm(ps[:, 1, E:2 * E], before, sel[:, 1], start=False, stop=True)
                mm(ps[0:1, 1, 2 * E:3 * E], ones[:, 0:1], sel[:, 0], start=True, stop=False)
                mm(ps[0:1, 1, 2 * E:3 * E], ones[:, 0:1], sel[:, 1], start=False, stop=True).then_inc(R.pos, 1)
                pe.wait_ge(R.xp, C.xp + T)
                round_(main, l)
                pe.wait_ge(R.over, C.over + 1)
                most = pe.value_load(over[0:1, 0:1], min_val=0, max_val=S)
                with pe.If(most > SLOTS):
                    with pe.Fori(0, ROUNDS - 1) as rho:
                        round_(rounds[1 + l], rho)

        @block.scalar
        def _(act):
            copy = nc.scalar.copy

            def transposed(dst, signal, at, done):
                for m in (0, 2):
                    act.wait_ge(signal, at + m + 1)
                    copy(dst[:, 2 * m:2 * m + 2, :], ps[:, m, :].rearrange("p (j t) -> p j t", j=2)).then_inc(done, 1)

            def tr_copy(l, r):
                B = base[l]
                act.wait_ge(L.tr, B.tr + r + 1)
                a = r % 2
                if l == 0 and r < 4:
                    dst, n = kT[:, 2 * (r // 2):2 * (r // 2) + 2, a * P:(a + 1) * P], 2
                elif l == 0:
                    dst, n = qT[:, 4 * (r // 2 - 2):4 * (r // 2 - 1), a * P:(a + 1) * P], 4
                else:
                    d = qT if r < 4 else kT
                    dst, n = d[:, 4 * (r // 2 % 2):4 * (r // 2 % 2) + 4, a * P:(a + 1) * P], 4
                copy(dst, ps[:, 4 + r % 2, 0:n * P].rearrange("p (b t) -> p b t", b=n)).then_inc(L.tr_copied, 1)

            def round_(rd, rho):
                act.wait_ge(rd.gathered, (PAIRS + 1) * rho + 1)
                copy(XeT[:, 0:4, :], ps[:, 2, :].rearrange("p (j c) -> p j c", j=4)).then_inc(rd.xe, 1)
                with act.Fori(0, PAIRS) as i:
                    n, g = PAIRS * rho + i, (PAIRS + 1) * rho + i
                    act.wait_ge(rd.gate_done, n + 1)
                    nc.scalar.activation(sg, ps[:, 0, :], ACT.Silu).then_inc(rd.silu, 1)
                    act.wait_ge(rd.gathered, g + 2)
                    copy(XeT[:, 0:4, :], ps[:, 2, :].rearrange("p (j c) -> p j c", j=4)).then_inc(rd.xe, 1)
                    act.wait_ge(rd.gt, n + 1)
                    copy(GT, ps[:, 1, 0:2 * P].rearrange("p (a c) -> p a c", a=T)).then_inc(rd.gt_copied, 1)
                    act.wait_ge(rd.y, 2 * n + 2)
                    copy(Y[:, UNIT:2 * UNIT], ps[:, 3, :]).then_inc(rd.y_a, 1)
                act.wait_ge(rd.comb, PAIRS * rho + PAIRS)
                act.sem_inc(round_over, 1)

            for l in range(2):
                B, C = base[l], rbase[l]
                transposed(xT, L.xt, B.xt, L.xt_sb)
                if l == 0:
                    for n in range(2):
                        act.wait_ge(L.proj, B.proj + n + 1)
                        copy(raw[:, n], bc(ps[:, n, :].rearrange("p (g c) -> p g c", g=2 * G), 2, 2)).then_inc(L.copied, 1)
                    for n in range(2, 6):
                        act.wait_ge(L.proj, B.proj + n + 1)
                        act.wait_ge(L.rope_mul, n - 1)
                        c = 256 * (n // 2 - 1)
                        copy(V[0][:, n % 2, c:c + 256], ps[:, n % 4, 256:512]).then_inc(L.copied, 1)
                    tr_copy(0, 0)
                    tr_copy(0, 1)
                    act.wait_ge(cmpw_used, 1)
                    act.wait_ge(hg_zero, 1)
                    for w in range(2):
                        r = slice(64 * w, 64 * w + G * NC)
                        nc.scalar.activation(hg[r, :], ps[r, 6, 0:CH], ACT.Gelu_apprx_tanh).then_inc(gelu, 1)
                    tr_copy(0, 2)
                    tr_copy(0, 3)
                    act.wait_ge(hg_t, 1)
                    copy(hgT, ps[:, 7, 0:2 * P].rearrange("p (k c) -> p k c", k=2)).then_inc(hgt_sb, 1)
                    tr_copy(0, 4)
                    tr_copy(0, 5)
                    act.wait_ge(L.proj, B.proj + 11)
                    nc.scalar.activation(gates, ps[:, 2, 0:128].rearrange("p (a h) -> p a h", a=T)[:, :, 0:3 * H],
                                         ACT.Sigmoid).then_inc(L.copied, 1)
                    act.wait_ge(kct, 1)
                    copy(kcT[:, 0:G * NC], ps[:, 7, 256:256 + G * NC]).then_inc(kct_sb, 1)
                    tr_copy(0, 6)
                    tr_copy(0, 7)
                else:
                    for r in range(8):
                        tr_copy(1, r)
                    for c in range(4):
                        act.wait_ge(L.proj, B.proj + 9 + c)
                        copy(V[1][:, c % 2, (c // 2) * UNIT:(c // 2 + 1) * UNIT], ps[:, c % 4, :]).then_inc(L.copied, 1)

                for m in range(len(ITEMS[l]) + 1):
                    if m < len(ITEMS[l]):
                        act.wait_ge(L.mx, B.mx + 2 * m + 2)
                        if m >= 2:
                            act.wait_ge(L.pt, B.pt + m - 1)
                        for t in range(T):
                            for a in range(2):
                                c = slice(t * P, t * P + (t + 1) * P)
                                last = nc.scalar.activation(Pb[m % 2][:, a, c], ps[:, 2 * (m % 2) + a, c], ACT.Exp,
                                                            bias=nmax[:, m % 2, t, a:a + 1],
                                                            accum_out=sums[:, m // 2, t, m % 2, a:a + 1])
                        last.then_inc(L.exp, 1)
                    if m >= 1:
                        act.wait_ge(L.pt, B.pt + m)
                        copy(PTb[(m - 1) % 2][:, 1, :], ps[:, 5, 0:384]).then_inc(L.pt_sb, 1)
                if l == 0:
                    for t in range(T):
                        act.wait_ge(cs_sub, t + 1)
                        nc.scalar.activation(Sc[:, t], Sc[:, t], ACT.Exp).then_inc(cs_exp, 1)
                    for t in range(T):
                        act.wait_ge(cp_t, t + 1)
                        copy(PTc[:, t, 0:4, :], ps[:, 4 - 4 * t, :].rearrange("p (j t) -> p j t", j=4)).then_inc(cp_sb, 1)
                transposed(OT, L.o_t, B.o_t, L.ot_sb)
                transposed(xT, R.xt, C.xt, R.xt_sb)
                act.wait_ge(R.logits, C.logits + 1)
                nc.scalar.activation(sc, ps[:, 0, 0:T * E].rearrange("p (a e) -> p a e", a=T), ACT.Sigmoid).then_inc(R.score, 1)
                nc.scalar.copy(Xp[:, 0], X[:, 0].rearrange("p (c j) -> p j c", j=KJ)).then_inc(R.xp, 1)
                round_(main, l)
                act.wait_ge(R.over, C.over + 1)
                most = act.value_load(over[0:1, 0:1], min_val=0, max_val=S)
                with act.If(most > SLOTS):
                    with act.Fori(0, ROUNDS - 1) as rho:
                        round_(rounds[1 + l], rho)

        @block.gpsimd
        def _(pool):
            tt = nc.gpsimd.tensor_tensor
            steps = [0]

            def step(ins):
                steps[0] += 1
                ins.then_inc(pool_step, 1)
                pool.wait_ge(pool_step, steps[0])

            def round_(rd, rho):
                one_hot = Pm.rearrange("p a e c -> p (a e) c")
                g0 = (PAIRS + 1) * rho
                pool.wait_ge(rd.onehot, g0 + 1)
                gp_of = lambda i: bc(gate[:, :, bass.ds(2 * i, 2)] if not isinstance(i, int) else gate[:, :, 2 * i:2 * i + 2], 3, SLOTS)
                tt(GP, Pm, gp_of(0), ALU.mult).then_inc(rd.gp, 1)
                with pool.Fori(0, PAIRS) as i:
                    n, g = PAIRS * rho + i, g0 + i
                    pool.wait_ge(rd.onehot, g + 2)
                    pool.wait_ge(rd.gt, n + 1)
                    tt(GP, Pm, gp_of(i + 1), ALU.mult).then_inc(rd.gp, 1)
                pool.wait_ge(rd.comb, PAIRS * rho + PAIRS)
                pool.wait_ge(rd.gp, g0 + PAIRS + 1)
                pool.sem_inc(round_over, 1)

            nc.gpsimd.memset(hg, 0.0).then_inc(hg_zero, 1)
            step(nc.gpsimd.memset(kcT, 0.0))
            step(nc.gpsimd.memset(vcb, 0.0))
            nc.gpsimd.memset(pos, -1.0)
            nc.gpsimd.memset(half, -0.5)
            step(nc.gpsimd.memset(gate, 0.0))
            pool.sem_inc(padded, 1)
            for l in range(2):
                B, C = base[l], rbase[l]
                for r in range(8):
                    pool.wait_ge(L.rope_mul, B.rope_mul + r + 1)
                    n = 256 if l == 0 and r < 4 else UNIT
                    tt(stage[r % 2][:, 0:n], stage[r % 2][:, 0:n], rope_b[r % 2][:, 0:n], ALU.add).then_inc(L.roped, 1)
                    if l == 0 and r == 5:
                        pool.wait_ge(kc_rope, 1)
                        n = G * NC
                        tt(kcr[0:n, :].rearrange("p (u c) -> p u c", u=2), bc(kca[0:n, :], 1, 2), bc(kcb[0:n, :], 1, 2),
                           ALU.add).then_inc(kc_add, 1)
                adds = 0
                if l == 0:
                    for q in range(4, 8):
                        for t in range(T):
                            pool.wait_ge(L.o_ev if t else L.o_half, q + 1)
                            h0, _, _ = heads(0, q)
                            o = O[:, t].rearrange("p (u h c) -> p u h c", u=4, h=4)[:, h0 // 4:h0 // 4 + 2, h0 % 4:h0 % 4 + 2, :]
                            src = otmp[q % 2][:, t * 256:(t + 1) * 256].rearrange("p (r a c) -> p a r c", r=2, a=2)
                            tt(o, o, src, ALU.add).then_inc(L.o_add, 1)
                    for t in range(T):
                        pool.wait_ge(cs_masked, t + 1)
                        pool.wait_ge(cs_max, t + 1)
                        tt(Sc[:, t], Sc[:, t], bc(cmax[:, t], 2, DH), ALU.subtract).then_inc(cs_sub, 1)
                    for t in range(T):
                        for hf in range(2):
                            adds += 1
                            pool.wait_ge(o_mul, adds)
                            o = O[:, t, hf * UNIT:(hf + 1) * UNIT]
                            tt(o, o, otmp[hf], ALU.add).then_inc(L.o_add, 1)
                for k in (2 * l, 2 * l + 1):
                    for t in range(T):
                        pool.wait_ge(N.stats, k * T + t + 1)
                        tt(rstd[:, t:t + 1], ve[:, t:t + 1], half[:, t:t + 1], ALU.pow).then_inc(N.rstd, 1)
                    for t in range(T):
                        pool.wait_ge(N.scaled, k * T + t + 1)
                        tt(X[:, t], X[:, t], lnw[:, 1], ALU.add).then_inc(N.x_ready, 1)
                    if k == 2 * l:
                        pool.wait_ge(N.x_ready, k * T + T)
                        nc.gpsimd.tensor_copy(Xp[:, 1], X[:, 1].rearrange("p (c j) -> p j c", j=KJ)).then_inc(R.xp, 1)
                        pool.wait_ge(R.table, C.table + 1)
                        round_(main, l)
                        pool.wait_ge(R.over, C.over + 1)
                        most = pool.value_load(over[0:1, 0:1], min_val=0, max_val=S)
                        with pool.If(most > SLOTS):
                            with pool.Fori(0, ROUNDS - 1) as rho:
                                round_(rounds[1 + l], rho)

        @block.vector
        def _(dve):
            tt, ts, copy = nc.vector.tensor_tensor, nc.vector.tensor_scalar, nc.vector.tensor_copy
            steps = [0]

            def step(ins):
                steps[0] += 1
                ins.then_inc(dve_step, 1)
                dve.wait_ge(dve_step, steps[0])

            def transposed(dst, signal, at, done):
                for m in (1, 3):
                    dve.wait_ge(signal, at + m + 1)
                    copy(dst[:, 2 * m:2 * m + 2, :], ps[:, m, :].rearrange("p (j t) -> p j t", j=2)).then_inc(done, 1)

            def rope(l, r):
                B = base[l]
                n = ROPE0[l] + r
                dve.wait_ge(L.proj, B.proj + n + 1)
                if r >= 2:
                    dve.wait_ge(L.tr, B.tr + r - 1)
                a = n % 2
                isq = r >= 4 if l == 0 else r < 4
                nh = 4 if l == 0 and r < 4 else 8
                cos = const("cosq" if isq else "cosk")[:, a * DH:(a + 1) * DH]
                sin = const("sinq" if isq else "sink")[:, a * DH:(a + 1) * DH]
                src, to, to_b = ps[:, n % 4, 0:nh * DH], stage[r % 2][:, 0:nh * DH], rope_b[r % 2][:, 0:nh * DH]
                if l == 0 and nh == 8:
                    src = src.rearrange("p (a i c) -> p a i c", a=2, i=4)
                    to, to_b = (v.rearrange("p (i a c) -> p a i c", a=2, i=4) for v in (to, to_b))
                else:
                    src, to, to_b = (v.rearrange("p (h c) -> p h c", h=nh) for v in (src, to, to_b))
                rope_mul(src, to, to_b, cos, sin).then_inc(L.rope_mul, 1)

            def rope_mul(src, to, to_b, cos, sin):
                def like(v, m):
                    for n in src.shape[1:-1]:
                        v = v.unsqueeze(1)
                    return v.to_broadcast(list(src.shape[:-1]) + [m])
                tt(to, src, like(cos, DH), ALU.mult)
                tt(to_b[..., 0:32], src[..., 32:64], like(sin[:, 0:32], 32), ALU.mult)
                return tt(to_b[..., 32:64], src[..., 0:32], like(sin[:, 32:64], 32), ALU.mult)

            def attention_max(l, m):
                B = base[l]
                dve.wait_ge(L.s_done, B.s_done + m + 1)
                b = 2 * (m % 2)
                for t in range(T):
                    nc.vector.tensor_reduce(nmax[:, m % 2, t, :], ps[:, b:b + 2, t * P:t * P + (t + 1) * P],
                                            AX.X, ALU.max, negate=True).then_inc(L.mx, 1)

            def weigh(l, q):
                B = base[l]
                dve.wait_ge(L.pv, B.pv + 2 * q + 2)
                c = coef[:, q % 2]
                step(nc.vector.reciprocal(c, sums[:, q]))
                h0, sr, sa = heads(l, q)
                if l == 0:
                    br = q // 4
                    for t in range(T):
                        gt_ = gates[:, t, (1 + br) * H:(2 + br) * H].rearrange("p (u h) -> p u h", u=4)
                        last = tt(c[:, t], c[:, t],
                                  gt_[:, h0 // 4:h0 // 4 + 2, h0 % 4:h0 % 4 + 2].rearrange("p a r -> p r a"), ALU.mult)
                    step(last)
                first = l == 1 or q < 4
                if not first and q >= 6:
                    dve.wait_ge(L.o_add, B.o_add + 2 * (q - 5))
                for t in range(T):
                    src = ps[:, 6 + q % 2, t * 256:(t + 1) * 256]
                    if l == 1:
                        dst = O[:, t, h0 * DH:(h0 + 4) * DH].rearrange("p (g c) -> p g c", g=4)
                        last = tt(dst, src.rearrange("p (g c) -> p g c", g=4),
                                  bc(c[:, t].rearrange("p r a -> p (r a)"), 2, DH), ALU.mult)
                        last.then_inc(L.o_ev if t else L.o_half, 1)
                        continue
                    if first:
                        o = O[:, t].rearrange("p (u h c) -> p u h c", u=4, h=4)[:, h0 // 4:h0 // 4 + 2, h0 % 4:h0 % 4 + 2, :]
                        dst = o.rearrange("p a r c -> p r a c")
                    else:
                        dst = otmp[q % 2][:, t * 256:(t + 1) * 256].rearrange("p (r a c) -> p r a c", r=2, a=2)
                    last = tt(dst, src.rearrange("p (r a c) -> p r a c", r=2, a=2), bc(c[:, t], 3, DH), ALU.mult)
                    last.then_inc(L.o_ev if t else L.o_half, 1)

            def layer_norm(k, ready, counts, ln_in, ln_n):
                for t in range(T):
                    for w in range(2):
                        dve.wait_ge(ready, counts[t][w])
                        last = nc.vector.bn_stats(bst[:, t, w, :], ps[:, 4 + 2 * t + w, :])
                    step(last)
                    step(nc.vector.bn_aggr(mv[:, t], bst[:, t].rearrange("p w s -> p (w s)")))
                    ts(ve[:, t:t + 1], mv[:, t, 1:2], EPS, None, ALU.add).then_inc(N.stats, 1)
                dve.wait_ge(ln_in, ln_n)
                for t in range(T):
                    dve.wait_ge(N.rstd, k * T + t + 1)
                    step(ts(X[:, t].rearrange("p (w c) -> p w c", w=2), ps[:, 4 + 2 * t:6 + 2 * t, :],
                            mv[:, t, 0:1], rstd[:, t:t + 1], ALU.subtract, ALU.mult))
                    tt(X[:, t], X[:, t], lnw[:, 0], ALU.mult).then_inc(N.scaled, 1)

            def ranks(v, n, out_):
                c1 = cg[:, 0:n * EG * EG].rearrange("p (g i j) -> p g i j", i=EG, j=EG)
                c2 = ch[:, 0:n * EG * EG].rearrange("p (g i j) -> p g i j", i=EG, j=EG)
                other, own = bc(v, 2, EG), bc(v, 3, EG)
                low = bc(const("lower").rearrange("p (i j) -> p i j", i=EG), 1, n)
                tt(c1, other, own, ALU.is_gt)
                step(tt(c2, other, own, ALU.is_ge))
                step(tt(c2, c2, low, ALU.mult))
                step(tt(c1, c1, c2, ALU.max))
                step(nc.vector.tensor_reduce(out_, c1, AX.X, ALU.add))

            def routing(C):
                dve.wait_ge(R.score, C.score + 1)
                dve.wait_ge(s_in, 112)
                step(tt(bs, sc, bc(rb, 1, T), ALU.add))
                b3 = bs.rearrange("p a (g e) -> p (a g) e", e=EG)
                r3 = rank[:, :].rearrange("p (g e) -> p g e", e=EG)
                s3 = sel2[:, :].rearrange("p (g e) -> p g e", e=EG)
                ranks(b3, T * EG, r3)
                step(ts(s3, r3, 1.5, None, ALU.is_lt))
                c3 = ch[:, 0:T * E].rearrange("p (g e) -> p g e", e=EG)
                step(tt(c3, b3, s3, ALU.mult))
                step(nc.vector.tensor_reduce(gs, c3, AX.X, ALU.add))
                ranks(gs[:, :].rearrange("p (a g) -> p a g", a=T), T, rank[:, 0:T * EG].rearrange("p (a g) -> p a g", a=T))
                step(ts(gsel, rank[:, 0:T * EG], 0.5, None, ALU.is_lt))
                f = sel.rearrange("p a (g e) -> p (a g) e", e=EG)
                tt(f, s3, bc(gsel, 2, EG), ALU.mult).then_inc(R.sel, 1)
                dve.wait_ge(R.sel, C.sel + 1)
                w = ch[:, 0:T * E].rearrange("p (a e) -> p a e", a=T)
                step(tt(w, sc, sel, ALU.mult))
                step(nc.vector.tensor_reduce(wsum, w, AX.X, ALU.add))
                step(nc.vector.reciprocal(wsum, wsum))
                dve.wait_ge(padded, 1)
                step(tt(gate[:, :, 0:E], w, bc(wsum, 2, E), ALU.mult))
                dve.wait_ge(R.pos, C.pos + 1)
                nc.vector.tensor_reduce(over[0:1, 0:1], ps[0:1, 1, 2 * E:3 * E], AX.X, ALU.max).then_inc(R.over, 1)
                step(nc.vector.scalar_tensor_tensor(pos[:, :, 0:E], ps[:, 1, 0:T * E].rearrange("p (a e) -> p a e", a=T), 1.0,
                                                    sel, ALU.add, ALU.mult))
                ts(pos[:, :, 0:E], pos[:, :, 0:E], -1.0, None, ALU.add).then_inc(R.table, 1)
                dve.wait_ge(R.table, C.table + 1)

            def one_hot(i):
                src = pos[:, :, bass.ds(2 * i, 2)] if not isinstance(i, int) else pos[:, :, 2 * i:2 * i + 2]
                return tt(Pm, bc(bc(const("slot"), 1, 2), 1, T), bc(src, 3, SLOTS), ALU.is_equal)

            def round_(rd, rho, shift):
                g0 = (PAIRS + 1) * rho
                if shift:
                    ts(pos, pos, float(-SLOTS), None, ALU.add).then_inc(rd.shift, 1)
                    dve.wait_ge(rd.shift, rho + 1)
                one_hot(0).then_inc(rd.onehot, 1)
                dve.wait_ge(rd.gathered, g0 + 1)
                copy(XeT[:, 4:8, :], ps[:, 3, :].rearrange("p (j c) -> p j c", j=4)).then_inc(rd.xe, 1)
                with dve.Fori(0, PAIRS) as i:
                    n, g = PAIRS * rho + i, g0 + i
                    dve.wait_ge(rd.gp, g + 1)
                    dve.wait_ge(rd.gathered, g + 1)
                    one_hot(i + 1).then_inc(rd.onehot, 1)
                    dve.wait_ge(rd.silu, n + 1)
                    dve.wait_ge(rd.up_done, n + 1)
                    tt(hid, sg, ps[:, 1, :], ALU.mult).then_inc(rd.h, 1)
                    dve.wait_ge(rd.gathered, g + 2)
                    copy(XeT[:, 4:8, :], ps[:, 3, :].rearrange("p (j c) -> p j c", j=4)).then_inc(rd.xe, 1)
                    dve.wait_ge(rd.ht, n + 1)
                    copy(hT, ps[:, 0, :].rearrange("p (k c) -> p k c", k=FJ)).then_inc(rd.ht_sb, 1)
                    dve.wait_ge(rd.y, 2 * n + 1)
                    copy(Y[:, 0:UNIT], ps[:, 2, :]).then_inc(rd.y_d, 1)
                dve.wait_ge(rd.comb, PAIRS * rho + PAIRS)
                dve.wait_ge(rd.gp, g0 + PAIRS + 1)
                dve.sem_inc(round_over, 1)

            dve.wait_ge(c_in, 16)
            copy(identb[:, :], ident).then_inc(bconst, 1)
            copy(causalb[:, :], const("causal")).then_inc(bconst, 1)
            for l in range(2):
                B, C = base[l], rbase[l]
                transposed(xT, L.xt, B.xt, L.xt_sb)
                for r in range(2):
                    rope(l, r)
                if l == 0:
                    dve.wait_ge(s_in, 112)
                    for w in range(2):
                        for gp in range(2):
                            dve.wait_ge(kcvc_t, 2 * w + gp + 1)
                            for par in range(2):
                                h = slice(64 * par, 64 * par + 64)
                                src = ps[h, 4 + 2 * w + gp, :].rearrange("p (g n m) -> p g n m", g=2, m=2 * 8)
                                last = None
                                for half_ in range(2):
                                    s4 = src[:, :, half_:half_ + NC, par:16:2]
                                    d4 = stat_kv[w][h, 8 * half_:8 * half_ + 8, 2 * gp:2 * gp + 2, :].rearrange("p m g n -> p g n m")
                                    pp = bc(bc(posT[h, w, 8 * half_:8 * half_ + 8], 1, NC), 1, 2)
                                    last = tt(d4, s4, pp, ALU.add)
                                last.then_inc(stat_done, 1)
                for r in range(2, 6):
                    rope(l, r)
                if l == 0:
                    dve.wait_ge(w2_done, 1)
                    n = G * NC
                    rope_mul(ps[0:n, 6, 0:DH], kca[0:n, :], kcb[0:n, :], const("ccos")[0:n, :], const("csin")[0:n, :]
                             ).then_inc(kc_rope, 1)
                    dve.wait_ge(padded, 1)
                    copy(vcb[0:n, 0:DH], ps[0:n, 6, DH:2 * DH])
                    copy(vcb[64:64 + n, DH:2 * DH], ps[0:n, 6, DH:2 * DH]).then_inc(vc_done, 1)
                for r in range(6, 8):
                    rope(l, r)
                items = len(ITEMS[l])
                for m in range(items + 2):
                    if m < items:
                        attention_max(l, m)
                    if 1 <= m <= items:
                        dve.wait_ge(L.pt, B.pt + m)
                        copy(PTb[(m - 1) % 2][:, 0, :], ps[:, 4, 0:384]).then_inc(L.pt_sb, 1)
                    if m >= 3 and m % 2:
                        weigh(l, (m - 3) // 2)
                if l == 0:
                    for t in range(T):
                        dve.wait_ge(cs_done, t + 1)
                        for a in range(2):
                            src = ps[:, 2 * t + a, :].rearrange("p (g h k) -> p g h k", g=2, h=4)
                            msk = const("cmask").rearrange("p (a g b k) -> p a b g k", a=T, g=2, b=2)[:, t, a]
                            last = tt(Sc[:, t, 8 * a:8 * a + 8].rearrange("p (g h) k -> p g h k", g=2), src, bc(msk, 2, 4), ALU.add)
                        last.then_inc(cs_masked, 1)
                        dve.wait_ge(cs_masked, t + 1)
                        nc.vector.tensor_reduce(cmax[:, t], Sc[:, t], AX.X, ALU.max).then_inc(cs_max, 1)
                    for t in range(T):
                        dve.wait_ge(cs_exp, t + 1)
                        step(nc.vector.tensor_reduce(csum[:, t], Sc[:, t], AX.X, ALU.add))
                        msk = const("cmask").rearrange("p (a g k) -> p a g k", a=T, g=G)[:, t]
                        for g in range(G):
                            at = 8 * (g % 2) + 4 * (g // 2)
                            s3 = Sc[:, t, at:at + 4]
                            last = nc.vector.scalar_tensor_tensor(s3, bc(msk[:, g], 1, 4), -1.0, s3, ALU.is_ge, ALU.mult)
                        last.then_inc(cs_p, 1)
                        step(nc.vector.reciprocal(csum[:, t], csum[:, t]))
                        c4 = csum[:, t].rearrange("p (a g i) -> p a g i", a=2, g=2)
                        step(tt(c4, c4, gates[:, t, 0:H].rearrange("p (g a i) -> p a g i", g=2, a=2), ALU.mult))
                    for t in range(T):
                        dve.wait_ge(cp_t, t + 1)
                        copy(PTc[:, t, 4:8, :], ps[:, 5 - 4 * t, :].rearrange("p (j t) -> p j t", j=4)).then_inc(cp_sb2, 1)
                    for t in range(T):
                        dve.wait_ge(cpv, t + 1)
                        for hf in range(2):
                            dve.wait_ge(L.o_add, B.o_add + 8 if t == 0 else 8 + hf + 1)
                            b = (6 if t == 0 else 2) + hf
                            w4 = csum[:, t].rearrange("p (a g i) -> p g a i", a=2, g=2)[:, hf]
                            tt(otmp[hf].rearrange("p (a i c) -> p a i c", a=2, i=4), ps[:, b, :].rearrange("p (a i c) -> p a i c", a=2, i=4),
                               bc(w4, 3, DH), ALU.mult).then_inc(o_mul, 1)
                transposed(OT, L.o_t, B.o_t, L.ot_sb)
                layer_norm(2 * l, L.mix, [[B.mix + 1, B.mix + 3], [B.mix + 2, B.mix + 4]], L.ln_in, B.ln_in + 32)
                transposed(xT, R.xt, C.xt, R.xt_sb)
                routing(C)
                round_(main, l, False)
                most = dve.value_load(over[0:1, 0:1], min_val=0, max_val=S)
                with dve.If(most > SLOTS):
                    with dve.Fori(0, ROUNDS - 1) as rho:
                        round_(rounds[1 + l], rho, True)
                layer_norm(2 * l + 1, main.comb, [[PAIRS * (l + 1)] * 2] * 2, R.ln_in, C.ln_in + 32)


def kernel(**inputs):
    import concourse.bacc as bacc
    from concourse.bass_utils import run_bass_kernel_spmd

    a = {k: np.asarray(v) for k, v in inputs.items()}
    places = lambda p: np.ascontiguousarray(p[0].reshape(CL // 2, 2 * DH).T)
    arrays = {
        "x": a["x"][0], "consts": constants(), "w_in0": a["nsa_w_in"][0], "w_out0": a["nsa_w_out"][0],
        "cmp_kw1": a["nsa_cmp_k_w1"][0], "cmp_kw2": a["nsa_cmp_k_w2"][0],
        "cmp_vw1": a["nsa_cmp_v_w1"][0], "cmp_vw2": a["nsa_cmp_v_w2"][0],
        "cmp_kpos": places(a["nsa_cmp_k_pos"]), "cmp_vpos": places(a["nsa_cmp_v_pos"]),
        "w_in1": a["moba_w_in"][0], "w_out1": a["moba_w_out"][0],
        "router_w": a["router_w"], "router_b": a["router_bias"].reshape(1, E),
        "w_gate": a["moe_w_gate"], "w_up": a["moe_w_up"], "w_down": a["moe_w_down"],
        "ln_g": a["ln_g"], "ln_b": a["ln_b"],
    }
    nc = bacc.Bacc("TRN2", target_bir_lowering=False, num_devices=1)
    feed, args = {}, []
    for name, v in arrays.items():
        v = np.ascontiguousarray(v)
        feed[f"in_{name}"] = v
        args.append(nc.dram_tensor(f"in_{name}", v.shape, mybir.dt.from_np(v.dtype), kind="ExternalInput").ap())
    args.append(nc.dram_tensor("out", (S, D), F32, kind="ExternalOutput").ap())
    build(nc, *args)
    r = run_bass_kernel_spmd(nc, [feed], core_ids=[0])
    return r.results[0]["out"].reshape(1, S, D)
```

```python
from collections import namedtuple
from contextlib import ExitStack

import numpy as np
import concourse.bass as bass
from concourse import mybir

F32 = mybir.dt.float32
BF16 = mybir.dt.bfloat16
I32 = mybir.dt.int32
ALU = mybir.AluOpType
ACT = mybir.ActivationFunctionType
AX = mybir.AxisListType

P = 128
D, S = 1024, 256
T = S // P
KJ = D // P
H, DH = 16, 64
G, HPG = 4, 4
UNIT = 512
NEG = -1e30
ALPHA = 4.0 ** 0.25
EPS = 1e-5
CL, CS = 32, 16
NC = (S - CL) // CS + 1
CH = 256
E, EG = 16, 4
FE = 512
FJ = FE // P
PAIRS = E // 2
SLOTS = 64
ROUNDS = S // SLOTS
RING = 6

CONST = {}
_at = 0
for _name, _n in (("ident", P), ("alphai", P), ("causal", P), ("before", P), ("ones", P),
                  ("cosq", T * DH), ("sinq", T * DH), ("cosk", T * DH), ("sink", T * DH),
                  ("cmask", T * G * DH), ("ccos", DH), ("csin", DH), ("slot", SLOTS), ("lower", EG * EG), ("valid", T)):
    CONST[_name] = (_at, _n)
    _at += _n
NCONST = _at


def constants():
    c = np.zeros((P, NCONST), np.float32)

    def put(name, a):
        at, n = CONST[name]
        c[:a.shape[0], at:at + n] = a.reshape(a.shape[0], n)

    p = np.arange(P)
    put("ident", np.eye(P))
    put("alphai", np.eye(P) * ALPHA)
    put("causal", np.where(p[None, :] > p[:, None], NEG, 0.0))
    put("before", (p[:, None] < p[None, :]) * 1.0)
    put("ones", np.ones((P, P)))
    f = np.float32
    inv = f(1.0) / (f(10000.0) ** (np.arange(0, DH, 2, dtype=f) / f(DH)))

    def rope(pos):
        ang = pos.astype(f)[:, None] * inv[None, :]
        cos, sin = np.cos(ang), np.sin(ang)
        return np.concatenate([cos, cos], 1), np.concatenate([-sin, sin], 1)

    cos, sin = rope(np.arange(S))
    tiles = lambda a: a.reshape(T, P, -1).transpose(1, 0, 2)
    put("cosk", tiles(cos))
    put("sink", tiles(sin))
    put("cosq", tiles(cos * f(DH ** -0.5)))
    put("sinq", tiles(sin * f(DH ** -0.5)))
    end = np.arange(NC) * CS + CL - 1
    cos, sin = rope(end)
    put("ccos", np.tile(cos, (G, 1)))
    put("csin", np.tile(sin, (G, 1)))
    m = np.full((S, G, DH), NEG, f)
    for g in range(G):
        m[:, g, g * NC:(g + 1) * NC] = np.where(end[None, :] <= np.arange(S)[:, None], 0.0, NEG)
    put("cmask", tiles(m.reshape(S, G * DH)))
    put("valid", tiles((np.arange(S) >= CL - 1)[:, None] * 1.0))
    put("slot", np.broadcast_to(np.arange(SLOTS), (P, SLOTS)))
    put("lower", np.broadcast_to((np.arange(EG)[None, :] < np.arange(EG)[:, None]) * 1.0, (P, EG, EG)))
    return c


def build(nc, x, consts, w_in0, w_out0, cmp_kw1, cmp_kw2, cmp_vw1, cmp_vw2, cmp_kpos, cmp_vpos,
          w_in1, w_out1, router_w, router_b, w_gate, w_up, w_down, ln_g, ln_b, out):
    ctx = ExitStack()
    with ctx:
        def sb(name, shape, dt=F32):
            return ctx.enter_context(nc.sbuf_tensor(name, shape, dt))

        def sem(name):
            return ctx.enter_context(nc.semaphore(name))

        ring = sb("ring", [P, RING, KJ * UNIT])
        area = sb("area", [P, 2, KJ, UNIT])
        cst = sb("cst", [P, NCONST])
        X = sb("X", [P, T, D])
        R1 = sb("R1", [P, T * D])
        R2 = sb("R2", [P, T * D])
        R3 = sb("R3", [P, T * D])
        R4 = sb("R4", [P, T * D])
        R5 = sb("R5", [P, 3 * D])
        R6 = sb("R6", [P, 3 * D])
        small = sb("small", [P, 1024])
        wgt = sb("wgt", [P, KJ, 3 * H])
        rw = sb("rw", [P, KJ, E])
        identb = sb("identb", [P, P], BF16)
        causalb = sb("causalb", [P, P], BF16)
        cmaskb = sb("cmaskb", [P, T, G, DH], BF16)
        over = sb("over", [1, 2], I32)
        ps = ctx.enter_context(nc.psum_tensor("ps", [P, 8, 512], F32))

        def const(name):
            at, n = CONST[name]
            return cst[:, at:at + n]

        ident = const("ident")
        used = [0]

        def tiny(n):
            used[0] += n
            assert used[0] <= 1024
            return small[:, used[0] - n:used[0]]

        xT = R1[:, :].rearrange("p (j t) -> p j t", j=KJ)
        qT = R2[:, :].rearrange("p (j t) -> p j t", j=KJ)
        OT = xT
        xTr = R3[:, :].rearrange("p (j t) -> p j t", j=KJ)
        Xp = R2[:, :].rearrange("p (a j c) -> p a j c", a=T, j=KJ)
        XeT = R3[:, 0:KJ * P].rearrange("p (j c) -> p j c", j=KJ)
        Y = R3[:, D:2 * D]
        stage = [R6[:, n * UNIT:(n + 1) * UNIT] for n in range(2)]
        rope_b = [R6[:, (2 + n) * UNIT:(3 + n) * UNIT] for n in range(2)]
        Pb = [R5[:, n * 768:(n + 1) * 768] for n in range(3)]
        PTb = [R6[:, n * 768:(n + 1) * 768].rearrange("p (a k) -> p a k", a=2) for n in range(2)]
        lnw = R5[:, 0:2 * D].rearrange("p (w c) -> p w c", w=2)
        stat_kv = [R5[:, n * 960:(n + 1) * 960].rearrange("p (m g n) -> p m g n", m=CL // 2, g=G) for n in range(2)]
        raw = R2[:, :].rearrange("p (a g u c) -> p a g u c", a=T, g=2 * G, u=2)
        hg = R4[:, D:D + CH]
        hgT = R4[:, D + 256:D + 512].rearrange("p (k c) -> p k c", k=2)
        w2 = R4[:, D + 512:D + 768].rearrange("p (w k c) -> p w k c", w=2, k=2)
        kcT = R4[:, D + 768:D + 832]
        vc = R4[:, D + 832:D + 896]
        kca = R3[:, D:D + 64]
        kcb = R3[:, D + 64:D + 128]
        kcr = R3[:, D + 128:D + 256]
        hid = R4[:, 0:FE]
        sg = R4[:, FE:2 * FE]
        hT = R4[:, 2 * FE:3 * FE].rearrange("p (k c) -> p k c", k=FJ)
        Pm = R4[:, 1536:1792].rearrange("p (a e c) -> p a e c", a=T, e=2)
        GP = R4[:, 1792:2048].rearrange("p (a e c) -> p a e c", a=T, e=2)
        GT = R6[:, 0:256].rearrange("p (a c) -> p a c", a=T)

        gates = tiny(T * 3 * H).rearrange("p (a h) -> p a h", a=T)
        posT = tiny(2 * 16).rearrange("p (w m) -> p w m", w=2)
        sums = tiny(12).rearrange("p (b t a) -> p b t a", b=3, t=T)
        nmax = tiny(8).rearrange("p (b a h) -> p b a h", b=2, a=T)
        coef = tiny(12).rearrange("p (b t a) -> p b t a", b=3, t=T)
        bst = tiny(T * 12).rearrange("p (a h s) -> p a h s", a=T, h=2)
        mv = tiny(T * 2).rearrange("p (a s) -> p a s", a=T)
        ve = tiny(T)
        half = tiny(T)
        rstd = tiny(T)
        rb = tiny(E)
        sc = tiny(T * E).rearrange("p (a e) -> p a e", a=T)
        bs = tiny(T * E).rearrange("p (a e) -> p a e", a=T)
        cg = tiny(T * E * EG)
        ch = tiny(T * E * EG)
        rank = tiny(T * E)
        sel2 = tiny(T * E)
        gs = tiny(T * EG)
        gsel = tiny(T * EG)
        sel = tiny(T * E).rearrange("p (a e) -> p a e", a=T)
        wsum = tiny(T)
        EP = E + 2
        pos = tiny(T * EP).rearrange("p (a e) -> p a e", a=T)
        gate = tiny(T * EP).rearrange("p (a e) -> p a e", a=T)

        x_in, ident_in, c_in, s_in = sem("x_in"), sem("ident_in"), sem("c_in"), sem("s_in")
        cmpw_in = sem("cmpw_in")
        area_in = [sem("area_in0"), sem("area_in1")]
        cmpw_used = sem("cmpw_used")
        bconst = sem("bconst")
        out_done = sem("out_done")
        padded, round_over = sem("padded"), sem("round_over")
        dve_step, pool_step = sem("dve_step"), sem("pool_step")
        LS = namedtuple("LS", "xt xt_sb proj rope_mul roped copied tr tr_copied s_done mx exp coef scaled "
                              "pt pt_sb pv ot_sb mix ln_in")
        L = LS(*(sem(n) for n in LS._fields))
        base = [LS(*[0] * len(LS._fields)),
                LS(xt=4, xt_sb=4, proj=11, rope_mul=8, roped=8, copied=7, tr=8, tr_copied=8, s_done=24, mx=24, exp=24,
                   coef=24, scaled=24, pt=24, pt_sb=48, pv=24, ot_sb=8, mix=4, ln_in=32)]
        kcvc_t, stat_done, h_done, gelu, hg_t, hgt_sb, w2_done, kc_rope, kc_add, vc_done, kct, kct_sb, hg_zero = (
            sem(n) for n in "kcvc_t stat_done h_done gelu hg_t hgt_sb w2_done kc_rope kc_add vc_done kct kct_sb hg_zero".split())
        LN = namedtuple("LN", "stats rstd x_ready")
        N = LN(*(sem(f"ln_{n}") for n in LN._fields))

        def ready(k, t, w):
            return 2 * (k * T + t) + w + 1

        RT = namedtuple("RT", "xt xt_sb logits score sel pos table over xp ln_in")
        R = RT(*(sem(f"route_{n}") for n in RT._fields))
        rbase = [RT(*[0] * len(RT._fields)), RT(4, 4, 1, 1, 1, 1, 1, 1, T, 32)]
        RD = namedtuple("RD", "w gate_done up_done gathered onehot gp silu h xe gt gt_copied ht ht_sb "
                              "y y_d y_a comb shift")
        rounds = [RD([sem(f"w{s}_{k}") for s in range(3)], *(sem(f"{n}_{k}") for n in RD._fields[1:]))
                  for k in ("main", "more0", "more1")]
        main = rounds[0]

        NSA_COLS = [1024, 1536, 2048, 0, 512]
        ROPE0 = [2, 0]
        ROPED = [8, 8]
        LAST = [11, 12]
        AREA0 = [0, 7]
        OUT0 = [5, 13]

        def ropes(l, n):
            return max(0, min(n + 1 - ROPE0[l], ROPED[l]))

        def copies(l, n):
            return min(n + 1, 6) + (n >= 10) if l == 0 else max(0, n + 1 - 8)

        ITEMS = [[(jq, br, 2 * (br - 1) + jq // 4, [256 * (br - 1) + 64 * (2 * (jq // 4) + a) for a in range(2)])
                  for jq in range(H // 2) for br in (1, 2, 0)],
                 [(j, 1, j, [128 * j + 64 * a for a in range(2)]) for j in range(H // 2)]]
        BRANCHES = [3, 1]

        block = ctx.enter_context(nc.Block())

        @block.sync
        def _(sp):
            def unit_src(u):
                if u < 5:
                    return w_in0[:, NSA_COLS[u]:NSA_COLS[u] + UNIT]
                if u < 7:
                    return w_out0[:, (u - 5) * UNIT:(u - 4) * UNIT]
                if u < 13:
                    return w_in1[:, (u - 7) * UNIT:(u - 6) * UNIT]
                return w_out1[:, (u - 13) * UNIT:(u - 12) * UNIT]

            def load_unit(u):
                if 2 <= u < 7:
                    sp.wait_ge(L.proj, 2 * (u - 1))
                elif 7 <= u < 9:
                    sp.wait_ge(L.mix, u - 4)
                elif u >= 9:
                    sp.wait_ge(L.proj, base[1].proj + 2 * (u - 8))
                sp.dma_start(area[:, u % 2], unit_src(u).rearrange("(j p) n -> p j n", p=P)).then_inc(area_in[u % 2], 16)

            def load_slot(rd, l, i, s):
                w = (w_gate, w_up, w_down)[s // 2]
                src = w[l, bass.ds(i, 1)] if not isinstance(i, int) else w[l, i:i + 1]
                if s < 4:
                    sp.dma_start(ring[:, s], src.rearrange("a (p j) n -> p (a j n)", p=P)).then_inc(rd.w[s // 2], 16)
                else:
                    sp.dma_start(ring[:, s].rearrange("p (k n) -> p k n", k=FJ),
                                 src.rearrange("a (k p) n -> p (a k) n", p=P)).then_inc(rd.w[s // 2], 16)

            def load_ln(k, signal):
                l, s = k // 2, k % 2
                sp.dma_start(lnw[:, 0], ln_g[l, s:s + 1].to_broadcast([P, D])).then_inc(signal, 16)
                sp.dma_start(lnw[:, 1], ln_b[l, s:s + 1].to_broadcast([P, D])).then_inc(signal, 16)

            def rest_of_round(rd, l, rho):
                with sp.Fori(1, PAIRS) as i:
                    n, n2 = sp.snap(i + PAIRS * rho), sp.snap(2 * i + 2 * PAIRS * rho)
                    experts = [sp.snap(2 * i), sp.snap(2 * i + 1)]
                    for s in range(RING):
                        if s < 2:
                            sp.wait_ge(rd.gate_done, n)
                        elif s < 4:
                            sp.wait_ge(rd.up_done, n)
                        else:
                            sp.wait_ge(rd.y, n2)
                        load_slot(rd, l, experts[s % 2], s)

            sp.dma_start(X[:, :, :], x.rearrange("(a p) c -> p a c", p=P)).then_inc(x_in, 16)
            sp.dma_start(cst[:, 0:P], consts[:, 0:P]).then_inc(ident_in, 16)
            load_unit(0)
            sp.dma_start(cst[:, P:], consts[:, P:]).then_inc(c_in, 16)
            load_unit(1)
            for s, (w2_, pos_) in enumerate(((cmp_kw2, cmp_kpos), (cmp_vw2, cmp_vpos))):
                sp.dma_start(w2[:, s], w2_.rearrange("(k p) n -> p k n", p=P)).then_inc(s_in, 16)
                sp.dma_start(posT[:, s], pos_).then_inc(s_in, 16)
            sp.dma_start(wgt[:, :, :], w_in0[:, 2560:2608].rearrange("(j p) n -> p j n", p=P)).then_inc(s_in, 16)
            sp.dma_start(rw[:, :, :], router_w.rearrange("(j p) n -> p j n", p=P)).then_inc(s_in, 16)
            sp.dma_start(rb, router_b.to_broadcast([P, E])).then_inc(s_in, 16)
            for s, w in ((4, cmp_kw1), (5, cmp_vw1)):
                sp.dma_start(ring[:, s].rearrange("p (m n) -> p m n", m=CL // 2),
                             w.rearrange("(m p) n -> p m n", p=P)).then_inc(cmpw_in, 16)
            load_slot(main, 0, 0, 0)
            load_unit(2)
            load_slot(main, 0, 1, 1)
            load_unit(3)
            load_slot(main, 0, 0, 2)
            load_unit(4)
            load_slot(main, 0, 1, 3)
            sp.wait_ge(cmpw_used, 1)
            load_slot(main, 0, 0, 4)
            load_slot(main, 0, 1, 5)
            load_unit(5)
            load_unit(6)
            for l in range(2):
                B, C, extra = base[l], rbase[l], rounds[1 + l]
                sp.wait_ge(L.pt, B.pt + len(ITEMS[l]))
                load_ln(2 * l, L.ln_in)
                if l == 0:
                    load_unit(7)
                    load_unit(8)
                sp.wait_ge(N.x_ready, ready(2 * l, T - 1, 1))
                load_ln(2 * l + 1, R.ln_in)
                rest_of_round(main, l, l)
                sp.wait_ge(R.over, C.over + 1)
                most = sp.value_load(over[0:1, 0:1], min_val=0, max_val=S)
                with sp.If(most > SLOTS):
                    sp.wait_ge(main.comb, T * PAIRS * (l + 1))
                    with sp.Fori(0, ROUNDS - 1) as rho:
                        for s in range(RING):
                            load_slot(extra, l, s % 2, s)
                        rest_of_round(extra, l, rho)
                        sp.wait_ge(extra.comb, T * PAIRS * (rho + 1))
                        sp.sem_inc(round_over, 1)
                if l == 0:
                    for s in range(RING):
                        sp.wait_ge(main.gate_done if s < 2 else main.up_done if s < 4 else main.y,
                                   PAIRS if s < 4 else 2 * PAIRS)
                        load_slot(main, 1, s % 2, s)
                    for u in range(9, 15):
                        load_unit(u)
            for a in range(T):
                sp.wait_ge(N.x_ready, ready(3, a, 1))
                sp.dma_start(out[a * P:(a + 1) * P, :], X[:, a]).then_inc(out_done, 16)
            sp.wait_ge(out_done, 16 * T)

        def bc(ap, axis, n):
            ap = ap.unsqueeze(axis)
            shape = list(ap.shape)
            shape[axis] = n
            return ap.to_broadcast(shape)

        V = [R4[:, 0:D].rearrange("p (a c) -> p a c", a=T), R4[:, :].rearrange("p (a c) -> p a c", a=T)]
        kT = R3[:, :].rearrange("p (j t) -> p j t", t=S)
        AREA_IN = lambda u: (area_in[u % 2], 16 * (u // 2 + 1))

        @block.tensor
        def _(pe):
            mm, tp = nc.tensor.matmul, nc.tensor.transpose

            def transpose_tile(a, signal, wait):
                for w in range(2):
                    wait(w)
                    for jj in range(4):
                        j = 4 * w + jj
                        last = tp(ps[:, 2 * a + w, jj * P:(jj + 1) * P], X[:, a, j * P:(j + 1) * P], ident)
                    last.then_inc(signal, 1)

            def project(l, n):
                B = base[l]
                u = AREA0[l] + n // 2
                if n % 2 == 0:
                    pe.wait_ge(*AREA_IN(u))
                if n >= 4:
                    if ropes(l, n - 4):
                        pe.wait_ge(L.rope_mul, B.rope_mul + ropes(l, n - 4))
                    if copies(l, n - 4):
                        pe.wait_ge(L.copied, B.copied + copies(l, n - 4))
                a = n % 2
                for j in range(KJ):
                    last = mm(ps[:, n % 4, :], xT[:, j, a * P:(a + 1) * P], area[:, u % 2, j, :],
                              start=(j == 0), stop=(j == KJ - 1))
                last.then_inc(L.proj, 1)

            def transpose_roped(l, r):
                B = base[l]
                pe.wait_ge(L.roped, B.roped + r + 1)
                if r >= 2:
                    pe.wait_ge(L.tr_copied, B.tr_copied + r - 1)
                elif l == 0:
                    pe.wait_ge(stat_done, 8)
                narrow = l == 0 and r < 4
                for b in range(2 if narrow else 4):
                    st = stage[r % 2]
                    last = tp(ps[:, 4 + r % 2, b * P:(b + 1) * P], st[:, b * P:(b + 1) * P], ident)
                last.then_inc(L.tr, 1)

            def scores(l, m):
                B = base[l]
                jq, br, jk, _ = ITEMS[l][m]
                if m == 0:
                    pe.wait_ge(L.tr_copied, B.tr_copied + 8)
                    pe.wait_ge(L.copied, B.copied + copies(l, LAST[l] - 1))
                    pe.wait_ge(bconst, 3)
                if m >= 2:
                    pe.wait_ge(L.exp, B.exp + m - 1)
                half_ = [slice(64 * a, 64 * a + 64) for a in range(2)]
                banks = [2 * (m % 2) + a for a in range(2)]
                for t in range(T):
                    at, n = (t * P, (t + 1) * P) if br else (t * DH, DH)
                    for a in range(2):
                        mm(ps[:, banks[a], at:at + n], qT[half_[a], jq, t * P:(t + 1) * P],
                           kT[half_[a], jk, 0:n] if br else kcT[half_[a], :], start=True, stop=False)
                    for a in range(2):
                        if br:
                            last = mm(ps[:, banks[a], at + t * P:at + n], identb[:, :], causalb[:, :], start=False, stop=True)
                        else:
                            last = mm(ps[:, banks[a], at:at + n], identb[:, :], cmaskb[:, t, 2 * (jq // 4) + a, :],
                                      start=False, stop=True)
                last.then_inc(L.s_done, 1)

            def transpose_probs(l, m):
                B = base[l]
                pe.wait_ge(L.scaled, B.scaled + m + 1)
                if m >= 1:
                    pe.wait_ge(L.pt_sb, B.pt_sb + 2 * m)
                if ITEMS[l][m][1]:
                    for a in range(2):
                        for b in range(3):
                            at = 384 * a + b * P
                            last = tp(ps[:, 4 + a, b * P:(b + 1) * P], Pb[m % 3][:, at:at + P], ident)
                else:
                    for t in range(T):
                        last = tp(ps[:, 4 + t, 0:P], Pb[m % 3][:, t * P:(t + 1) * P], ident)
                last.then_inc(L.pt, 1)

            def times_v(l, m):
                B = base[l]
                jq, br, _, cols = ITEMS[l][m]
                nb = BRANCHES[l]
                pe.wait_ge(L.pt_sb, B.pt_sb + 2 * m + 2)
                if m % nb == 0 and jq >= 2:
                    pe.wait_ge(L.ot_sb, B.ot_sb + jq - 1)
                if m == 0 and l == 0:
                    pe.wait_ge(kct_sb, 1)
                    pe.wait_ge(vc_done, 1)
                    pe.wait_ge(kc_rope, 1)
                first, end = m % nb == 0, m % nb == nb - 1
                o = ps[:, 6 + jq % 2, 0:S]
                pt = PTb[m % 2]
                if br:
                    for a in range(2):
                        last = mm(o[64 * a:64 * a + 64, :], V[l][:, 0, cols[a]:cols[a] + DH], pt[:, a, 0:2 * P],
                                  start=first, stop=False, skip_group_check=True)
                    for a in range(2):
                        last = mm(o[64 * a:64 * a + 64, P:2 * P], V[l][:, 1, cols[a]:cols[a] + DH], pt[:, a, 2 * P:3 * P],
                                  start=False, stop=end, skip_group_check=True)
                else:
                    for a in range(2):
                        h = slice(64 * a, 64 * a + 64)
                        last = mm(o[h, :].rearrange("p (t c) -> p t c", t=T), vc[h, :], pt[h, :, 0:P],
                                  start=False, stop=end, skip_group_check=True)
                last.then_inc(L.pv, 1)

            def attention(l):
                n = len(ITEMS[l])
                for m in range(n + 3):
                    if m < n:
                        scores(l, m)
                    if 2 <= m < n + 2:
                        transpose_probs(l, m - 2)
                    if m >= 3:
                        times_v(l, m - 3)

            def mix_out(l):
                B = base[l]
                for a in range(T):
                    if a:
                        pe.wait_ge(L.ot_sb, B.ot_sb + H // 2)
                    for w in range(2):
                        seed(a, w, False)
                for a in range(T):
                    for w in range(2):
                        u = OUT0[l] + w
                        if a == 0:
                            pe.wait_ge(*AREA_IN(u))
                        if a and w:
                            transpose_tile(0, R.xt, lambda w: pe.wait_ge(N.x_ready, ready(2 * l, 0, w)))
                        for j in range(KJ):
                            last = mm(ps[:, 4 + 2 * a + w, :], OT[:, j, a * P:(a + 1) * P], area[:, u % 2, j, :],
                                      start=False, stop=(j == KJ - 1), skip_group_check=True)
                        last.then_inc(L.mix, 1)

            def seed(a, w, stop):
                mm(ps[:, 4 + 2 * a + w, :], const("alphai"), X[:, a, w * UNIT:(w + 1) * UNIT],
                   start=True, stop=stop, skip_group_check=True)

            def logits(l, a):
                pe.wait_ge(R.xt_sb, rbase[l].xt_sb + 2 * a + 2)
                for j in range(KJ):
                    last = mm(ps[:, 0, a * E:(a + 1) * E], xTr[:, j, a * P:(a + 1) * P], rw[:, j, :],
                              start=(j == 0), stop=(j == KJ - 1))
                return last

            def gather(rd):
                for j in range(KJ):
                    for a in range(T):
                        last = mm(ps[:, 2 + j // 4, (j % 4) * P:(j % 4 + 1) * P], Xp[:, a, j, :],
                                  Pm[:, a].rearrange("p e c -> p (e c)"), start=(a == 0), stop=(a == T - 1))
                last.then_inc(rd.gathered, 1)

            def round_(rd, rho):
                pe.wait_ge(rd.onehot, (PAIRS + 1) * rho + 1)
                gather(rd)
                with pe.Fori(0, PAIRS) as i:
                    n, g = PAIRS * rho + i, (PAIRS + 1) * rho + i
                    pe.wait_ge(rd.xe, 2 * g + 2)
                    for w, done in ((0, rd.gate_done), (1, rd.up_done)):
                        pe.wait_ge(rd.w[w], 32 * n + 32)
                        for j in range(KJ):
                            for e in range(2):
                                last = mm(ps[64 * e:64 * e + 64, w, :], XeT[:, j, 64 * e:64 * e + 64],
                                          ring[:, 2 * w + e, j * UNIT:(j + 1) * UNIT], start=(j == 0), stop=(j == KJ - 1))
                        last.then_inc(done, 1)
                    pe.wait_ge(rd.onehot, g + 2)
                    gather(rd)
                    pe.wait_ge(rd.gp, g + 1)
                    pe.wait_ge(rd.h, n + 1)
                    for a in range(T):
                        last = tp(ps[:, 1, a * P:(a + 1) * P], GP[:, a].rearrange("p e c -> p (e c)"), ident)
                    last.then_inc(rd.gt, 1)
                    for k in range(FJ):
                        last = tp(ps[:, 0, k * P:(k + 1) * P], hid[:, k * P:(k + 1) * P], ident)
                    last.then_inc(rd.ht, 1)
                    pe.wait_ge(rd.xe, 2 * g + 4)
                    pe.wait_ge(rd.ht_sb, n + 1)
                    pe.wait_ge(rd.w[2], 32 * n + 32)
                    for w in range(2):
                        for k in range(FJ):
                            for e in range(2):
                                last = mm(ps[64 * e:64 * e + 64, 2 + w, :], hT[:, k, 64 * e:64 * e + 64],
                                          ring[:, 4 + e, k * D + w * UNIT:k * D + (w + 1) * UNIT],
                                          start=(k == 0), stop=(k == FJ - 1))
                        last.then_inc(rd.y, 1)
                    pe.wait_ge(rd.gt_copied, n + 1)
                    pe.wait_ge(rd.y_d, n + 1)
                    pe.wait_ge(rd.y_a, n + 1)
                    for a in range(T):
                        for w in range(2):
                            last = mm(ps[:, 4 + 2 * a + w, :], GT[:, a, :], Y[:, w * UNIT:(w + 1) * UNIT],
                                      start=False, stop=True, skip_group_check=True)
                        last.then_inc(rd.comb, 1)

            pe.wait_ge(ident_in, 16)
            for l in range(2):
                B, C = base[l], rbase[l]
                for a in range(T):
                    transpose_tile(a, L.xt, (lambda w: pe.wait_ge(x_in, 16)) if l == 0 else
                                   (lambda w: pe.wait_ge(N.x_ready, ready(1, a, w))))
                    pe.wait_ge(L.xt_sb, B.xt_sb + 2 * a + 2)
                    project(l, a)
                if l == 0:
                    for n in range(2, 4):
                        project(0, n)
                    pe.wait_ge(L.copied, B.copied + 2)
                    for w in range(2):
                        for g in range(G):
                            for a in range(T):
                                blk = raw[:, a, G * w + g].rearrange("p u c -> p (u c)")
                                last = tp(ps[:, 4 + 2 * w + g // 2, (g % 2) * S + a * P:(g % 2) * S + (a + 1) * P], blk, ident)
                            if g % 2:
                                last.then_inc(kcvc_t, 1)
                    project(0, 4)
                    project(0, 5)
                    transpose_roped(0, 0)
                    transpose_roped(0, 1)
                    pe.wait_ge(cmpw_in, 32)
                    pe.wait_ge(stat_done, 8)
                    for m in range(CL // 2):
                        for w in range(2):
                            last = mm(ps[64 * w:64 * w + G * NC, 6, 0:CH], stat_kv[w][:, m].rearrange("p g n -> p (g n)"),
                                      ring[:, 4 + w, m * CH:(m + 1) * CH], start=(m == 0), stop=(m == CL // 2 - 1))
                    last.then_inc(cmpw_used, 1)
                    project(0, 6)
                    project(0, 7)
                    transpose_roped(0, 2)
                    transpose_roped(0, 3)
                    pe.wait_ge(gelu, 2)
                    for k in range(2):
                        last = tp(ps[:, 7, k * P:(k + 1) * P], hg[:, k * P:(k + 1) * P], ident)
                    last.then_inc(hg_t, 1)
                    project(0, 8)
                    project(0, 9)
                    pe.wait_ge(hgt_sb, 1)
                    pe.wait_ge(s_in, 112)
                    for w in range(2):
                        for k in range(2):
                            last = mm(ps[0:G * NC, 6, w * DH:(w + 1) * DH], hgT[:, k, 64 * w:64 * w + G * NC],
                                      w2[:, w, k, :], start=(k == 0), stop=(k == 1))
                    last.then_inc(w2_done, 1)
                    transpose_roped(0, 4)
                    transpose_roped(0, 5)
                    pe.wait_ge(L.rope_mul, B.rope_mul + ropes(0, 6))
                    for a in range(T):
                        for j in range(KJ):
                            last = mm(ps[:, 10 % 4, a * 64:a * 64 + 3 * H], xT[:, j, a * P:(a + 1) * P], wgt[:, j, :],
                                      start=(j == 0), stop=(j == KJ - 1))
                    last.then_inc(L.proj, 1)
                    pe.wait_ge(kc_add, 1)
                    tp(ps[:, 7, 256:256 + G * NC], kcr[0:G * NC, :], ident[0:G * NC, 0:G * NC]).then_inc(kct, 1)
                    transpose_roped(0, 6)
                    transpose_roped(0, 7)
                else:
                    for n in range(2, 4):
                        project(1, n)
                    for r in range(0, 8, 2):
                        transpose_roped(1, r)
                        transpose_roped(1, r + 1)
                        project(1, r + 4)
                        project(1, r + 5)
                attention(l)
                mix_out(l)
                logits(l, 0)
                for w in range(2):
                    seed(0, w, True)
                transpose_tile(1, R.xt, lambda w: pe.wait_ge(N.x_ready, ready(2 * l, 1, w)))
                logits(l, 1).then_inc(R.logits, 1)
                for w in range(2):
                    seed(1, w, True)
                pe.wait_ge(R.sel, C.sel + 1)
                before, ones = const("before"), const("ones")
                mm(ps[:, 1, 0:E], before, sel[:, 0], start=True, stop=True)
                mm(ps[:, 1, E:2 * E], ones, sel[:, 0], start=True, stop=False)
                mm(ps[:, 1, E:2 * E], before, sel[:, 1], start=False, stop=True)
                mm(ps[0:1, 1, 2 * E:3 * E], ones[:, 0:1], sel[:, 0], start=True, stop=False)
                mm(ps[0:1, 1, 2 * E:3 * E], ones[:, 0:1], sel[:, 1], start=False, stop=True).then_inc(R.pos, 1)
                pe.wait_ge(R.xp, C.xp + T)
                round_(main, l)
                pe.wait_ge(R.over, C.over + 1)
                most = pe.value_load(over[0:1, 0:1], min_val=0, max_val=S)
                with pe.If(most > SLOTS):
                    with pe.Fori(0, ROUNDS - 1) as rho:
                        round_(rounds[1 + l], rho)

        @block.scalar
        def _(act):
            copy = nc.scalar.copy

            def transposed(dst, a, signal, at, done):
                act.wait_ge(signal, at + 2 * a + 1)
                copy(dst[:, 0:4, a * P:(a + 1) * P], ps[:, 2 * a, :].rearrange("p (j t) -> p j t", j=4)).then_inc(done, 1)

            def tr_copy(l, r):
                B = base[l]
                act.wait_ge(L.tr, B.tr + r + 1)
                a = r % 2
                if l == 0 and r < 4:
                    dst, n = kT[:, 2 * (r // 2):2 * (r // 2) + 2, a * P:(a + 1) * P], 2
                elif l == 0:
                    dst, n = qT[:, 4 * (r // 2 - 2):4 * (r // 2 - 1), a * P:(a + 1) * P], 4
                else:
                    d = qT if r < 4 else kT
                    dst, n = d[:, 4 * (r // 2 % 2):4 * (r // 2 % 2) + 4, a * P:(a + 1) * P], 4
                copy(dst, ps[:, 4 + r % 2, 0:n * P].rearrange("p (b t) -> p b t", b=n)).then_inc(L.tr_copied, 1)

            def round_(rd, rho):
                act.wait_ge(rd.gathered, (PAIRS + 1) * rho + 1)
                copy(XeT[:, 0:4, :], ps[:, 2, :].rearrange("p (j c) -> p j c", j=4)).then_inc(rd.xe, 1)
                with act.Fori(0, PAIRS) as i:
                    n, g = PAIRS * rho + i, (PAIRS + 1) * rho + i
                    act.wait_ge(rd.gate_done, n + 1)
                    nc.scalar.activation(sg, ps[:, 0, :], ACT.Silu).then_inc(rd.silu, 1)
                    act.wait_ge(rd.gathered, g + 2)
                    copy(XeT[:, 0:4, :], ps[:, 2, :].rearrange("p (j c) -> p j c", j=4)).then_inc(rd.xe, 1)
                    act.wait_ge(rd.gt, n + 1)
                    copy(GT, ps[:, 1, 0:2 * P].rearrange("p (a c) -> p a c", a=T)).then_inc(rd.gt_copied, 1)
                    act.wait_ge(rd.y, 2 * n + 2)
                    copy(Y[:, UNIT:2 * UNIT], ps[:, 3, :]).then_inc(rd.y_a, 1)
                act.wait_ge(rd.comb, T * PAIRS * (rho + 1))
                act.sem_inc(round_over, 1)

            for l in range(2):
                B, C = base[l], rbase[l]
                for a in range(T):
                    transposed(xT, a, L.xt, B.xt, L.xt_sb)
                if l == 0:
                    for n in range(2):
                        act.wait_ge(L.proj, B.proj + n + 1)
                        copy(raw[:, n], bc(ps[:, n, :].rearrange("p (g c) -> p g c", g=2 * G), 2, 2)).then_inc(L.copied, 1)
                    for n in range(2, 6):
                        act.wait_ge(L.proj, B.proj + n + 1)
                        act.wait_ge(L.rope_mul, n - 1)
                        c = 256 * (n // 2 - 1)
                        copy(V[0][:, n % 2, c:c + 256], ps[:, n % 4, 256:512]).then_inc(L.copied, 1)
                    tr_copy(0, 0)
                    tr_copy(0, 1)
                    act.wait_ge(cmpw_used, 1)
                    act.wait_ge(hg_zero, 1)
                    for w in range(2):
                        r = slice(64 * w, 64 * w + G * NC)
                        nc.scalar.activation(hg[r, :], ps[r, 6, 0:CH], ACT.Gelu_apprx_tanh).then_inc(gelu, 1)
                    tr_copy(0, 2)
                    tr_copy(0, 3)
                    act.wait_ge(hg_t, 1)
                    copy(hgT, ps[:, 7, 0:2 * P].rearrange("p (k c) -> p k c", k=2)).then_inc(hgt_sb, 1)
                    tr_copy(0, 4)
                    tr_copy(0, 5)
                    act.wait_ge(L.proj, B.proj + 11)
                    nc.scalar.activation(gates, ps[:, 2, 0:128].rearrange("p (a h) -> p a h", a=T)[:, :, 0:3 * H],
                                         ACT.Sigmoid).then_inc(L.copied, 1)
                    act.wait_ge(kct, 1)
                    copy(kcT[:, 0:G * NC], ps[:, 7, 256:256 + G * NC]).then_inc(kct_sb, 1)
                    tr_copy(0, 6)
                    tr_copy(0, 7)
                else:
                    for r in range(8):
                        tr_copy(1, r)
                    for c in range(4):
                        act.wait_ge(L.proj, B.proj + 9 + c)
                        copy(V[1][:, c % 2, (c // 2) * UNIT:(c // 2 + 1) * UNIT], ps[:, c % 4, :]).then_inc(L.copied, 1)

                n = len(ITEMS[l])
                for m in range(n + 2):
                    if m < n:
                        br = ITEMS[l][m][1]
                        act.wait_ge(L.mx, B.mx + m + 1)
                        if m >= 3:
                            act.wait_ge(L.pt, B.pt + m - 2)
                        for t in range(T):
                            for a in range(2):
                                if br:
                                    c, w = t * P, (t + 1) * P
                                    to = Pb[m % 3][:, 384 * a + c:384 * a + c + w]
                                else:
                                    c, w = t * DH, DH
                                    to = Pb[m % 3][:, (2 * t + a) * DH:(2 * t + a + 1) * DH]
                                last = nc.scalar.activation(to, ps[:, 2 * (m % 2) + a, c:c + w], ACT.Exp,
                                                            bias=nmax[:, m % 2, t, a:a + 1],
                                                            accum_out=sums[:, m % 3, t, a:a + 1])
                        last.then_inc(L.exp, 1)
                    if m >= 2:
                        act.wait_ge(L.pt, B.pt + m - 1)
                        w = 384 if ITEMS[l][m - 2][1] else P
                        copy(PTb[m % 2][:, 1, 0:w], ps[:, 5, 0:w]).then_inc(L.pt_sb, 1)
                permuted = lambda a: nc.scalar.copy(Xp[:, a], X[:, a].rearrange("p (c j) -> p j c", j=KJ)).then_inc(R.xp, 1)
                transposed(xTr, 0, R.xt, C.xt, R.xt_sb)
                act.wait_ge(N.x_ready, ready(2 * l, 0, 1))
                permuted(0)
                transposed(xTr, 1, R.xt, C.xt, R.xt_sb)
                act.wait_ge(R.logits, C.logits + 1)
                nc.scalar.activation(sc, ps[:, 0, 0:T * E].rearrange("p (a e) -> p a e", a=T), ACT.Sigmoid).then_inc(R.score, 1)
                act.wait_ge(N.x_ready, ready(2 * l, 1, 1))
                permuted(1)
                round_(main, l)
                act.wait_ge(R.over, C.over + 1)
                most = act.value_load(over[0:1, 0:1], min_val=0, max_val=S)
                with act.If(most > SLOTS):
                    with act.Fori(0, ROUNDS - 1) as rho:
                        round_(rounds[1 + l], rho)

        @block.gpsimd
        def _(pool):
            tt = nc.gpsimd.tensor_tensor
            steps = [0]

            def step(ins):
                steps[0] += 1
                ins.then_inc(pool_step, 1)
                pool.wait_ge(pool_step, steps[0])

            def round_(rd, rho):
                one_hot = Pm.rearrange("p a e c -> p (a e) c")
                g0 = (PAIRS + 1) * rho
                pool.wait_ge(rd.onehot, g0 + 1)
                gp_of = lambda i: bc(gate[:, :, bass.ds(2 * i, 2)] if not isinstance(i, int) else gate[:, :, 2 * i:2 * i + 2], 3, SLOTS)
                tt(GP, Pm, gp_of(0), ALU.mult).then_inc(rd.gp, 1)
                with pool.Fori(0, PAIRS) as i:
                    n, g = PAIRS * rho + i, g0 + i
                    pool.wait_ge(rd.onehot, g + 2)
                    pool.wait_ge(rd.gt, n + 1)
                    tt(GP, Pm, gp_of(i + 1), ALU.mult).then_inc(rd.gp, 1)
                pool.wait_ge(rd.comb, T * PAIRS * (rho + 1))
                pool.wait_ge(rd.gp, g0 + PAIRS + 1)
                pool.sem_inc(round_over, 1)

            nc.gpsimd.memset(hg, 0.0).then_inc(hg_zero, 1)
            step(nc.gpsimd.memset(kcT, 0.0))
            step(nc.gpsimd.memset(vc, 0.0))
            nc.gpsimd.memset(pos, -1.0)
            nc.gpsimd.memset(half, -0.5)
            step(nc.gpsimd.memset(gate, 0.0))
            pool.sem_inc(padded, 1)
            for l in range(2):
                B, C = base[l], rbase[l]
                for r in range(8):
                    pool.wait_ge(L.rope_mul, B.rope_mul + r + 1)
                    n = 256 if l == 0 and r < 4 else UNIT
                    tt(stage[r % 2][:, 0:n], stage[r % 2][:, 0:n], rope_b[r % 2][:, 0:n], ALU.add).then_inc(L.roped, 1)
                    if l == 0 and r == 5:
                        pool.wait_ge(kc_rope, 1)
                        n = G * NC
                        tt(kcr[0:n, :].rearrange("p (u c) -> p u c", u=2), bc(kca[0:n, :], 1, 2), bc(kcb[0:n, :], 1, 2),
                           ALU.add).then_inc(kc_add, 1)
                for m in range(len(ITEMS[l])):
                    pool.wait_ge(L.coef, B.coef + m + 1)
                    c = coef[:, m % 3]
                    if ITEMS[l][m][1]:
                        p3 = Pb[m % 3].rearrange("p (a k) -> p a k", a=2)
                        tt(p3[:, :, 0:P], p3[:, :, 0:P], bc(c[:, 0], 2, P), ALU.mult)
                        last = tt(p3[:, :, P:3 * P], p3[:, :, P:3 * P], bc(c[:, 1], 2, 2 * P), ALU.mult)
                    else:
                        p4 = Pb[m % 3][:, 0:4 * DH].rearrange("p (t a k) -> p t a k", t=T, a=2)
                        last = tt(p4, p4, bc(c, 3, DH), ALU.mult)
                    last.then_inc(L.scaled, 1)
                for k in (2 * l, 2 * l + 1):
                    for t in range(T):
                        pool.wait_ge(N.stats, k * T + t + 1)
                        tt(rstd[:, t:t + 1], ve[:, t:t + 1], half[:, t:t + 1], ALU.pow).then_inc(N.rstd, 1)
                    if k == 2 * l:
                        pool.wait_ge(R.table, C.table + 1)
                        round_(main, l)
                        pool.wait_ge(R.over, C.over + 1)
                        most = pool.value_load(over[0:1, 0:1], min_val=0, max_val=S)
                        with pool.If(most > SLOTS):
                            with pool.Fori(0, ROUNDS - 1) as rho:
                                round_(rounds[1 + l], rho)

        @block.vector
        def _(dve):
            tt, ts, copy = nc.vector.tensor_tensor, nc.vector.tensor_scalar, nc.vector.tensor_copy
            stt = nc.vector.scalar_tensor_tensor
            steps = [0]

            def step(ins):
                steps[0] += 1
                ins.then_inc(dve_step, 1)
                dve.wait_ge(dve_step, steps[0])

            def transposed(dst, a, signal, at, done):
                dve.wait_ge(signal, at + 2 * a + 2)
                copy(dst[:, 4:8, a * P:(a + 1) * P], ps[:, 2 * a + 1, :].rearrange("p (j t) -> p j t", j=4)).then_inc(done, 1)

            def rope(l, r):
                B = base[l]
                n = ROPE0[l] + r
                dve.wait_ge(L.proj, B.proj + n + 1)
                if r >= 2:
                    dve.wait_ge(L.tr, B.tr + r - 1)
                a = n % 2
                isq = r >= 4 if l == 0 else r < 4
                nh = 4 if l == 0 and r < 4 else 8
                cos = const("cosq" if isq else "cosk")[:, a * DH:(a + 1) * DH]
                sin = const("sinq" if isq else "sink")[:, a * DH:(a + 1) * DH]
                src, to, to_b = ps[:, n % 4, 0:nh * DH], stage[r % 2][:, 0:nh * DH], rope_b[r % 2][:, 0:nh * DH]
                if l == 0 and nh == 8:
                    src = src.rearrange("p (a i c) -> p a i c", a=2, i=4)
                    to, to_b = (v.rearrange("p (i a c) -> p a i c", a=2, i=4) for v in (to, to_b))
                else:
                    src, to, to_b = (v.rearrange("p (h c) -> p h c", h=nh) for v in (src, to, to_b))
                rope_mul(src, to, to_b, cos, sin).then_inc(L.rope_mul, 1)

            def rope_mul(src, to, to_b, cos, sin):
                def like(v, m):
                    for n in src.shape[1:-1]:
                        v = v.unsqueeze(1)
                    return v.to_broadcast(list(src.shape[:-1]) + [m])
                tt(to, src, like(cos, DH), ALU.mult)
                tt(to_b[..., 0:32], src[..., 32:64], like(sin[:, 0:32], 32), ALU.mult)
                return tt(to_b[..., 32:64], src[..., 0:32], like(sin[:, 32:64], 32), ALU.mult)

            def attention_max(l, m):
                B = base[l]
                dve.wait_ge(L.s_done, B.s_done + m + 1)
                b = 2 * (m % 2)
                if ITEMS[l][m][1]:
                    for t in range(T):
                        last = nc.vector.tensor_reduce(nmax[:, m % 2, t, :], ps[:, b:b + 2, t * P:t * P + (t + 1) * P],
                                                       AX.X, ALU.max, negate=True)
                else:
                    last = nc.vector.tensor_reduce(nmax[:, m % 2].rearrange("p t a -> p a t"),
                                                   ps[:, b:b + 2, 0:2 * DH].rearrange("p a (t k) -> p a t k", t=T),
                                                   AX.X, ALU.max, negate=True)
                last.then_inc(L.mx, 1)

            def coefficients(l, m):
                B = base[l]
                jq, br, _, _ = ITEMS[l][m]
                dve.wait_ge(L.exp, B.exp + m + 1)
                if m >= 3:
                    dve.wait_ge(L.scaled, B.scaled + m - 2)
                c = coef[:, m % 3]
                last = nc.vector.reciprocal(c, sums[:, m % 3])
                if l == 0:
                    step(last)
                    h0 = 8 * (jq // 4) + jq % 4
                    g = gates[:, :, br * H:(br + 1) * H].rearrange("p t (u i) -> p t u i", i=4)
                    last = tt(c, c, g[:, :, h0 // 4:h0 // 4 + 2, h0 % 4], ALU.mult)
                last.then_inc(L.coef, 1)

            def layer_norm(k, t, signal, counts, ln_in, ln_n):
                for w in range(2):
                    dve.wait_ge(signal, counts[w])
                    last = nc.vector.bn_stats(bst[:, t, w, :], ps[:, 4 + 2 * t + w, :])
                step(last)
                step(nc.vector.bn_aggr(mv[:, t], bst[:, t].rearrange("p w s -> p (w s)")))
                ts(ve[:, t:t + 1], mv[:, t, 1:2], EPS, None, ALU.add).then_inc(N.stats, 1)
                dve.wait_ge(ln_in, ln_n)
                for w in range(2):
                    c = slice(w * UNIT, (w + 1) * UNIT)
                    last = stt(X[:, t, c], ps[:, 4 + 2 * t + w, :], mv[:, t, 0:1], lnw[:, 0, c], ALU.subtract, ALU.mult)
                    if w == 0:
                        first = steps[0] = steps[0] + 1
                    else:
                        steps[0] += 1
                    last.then_inc(dve_step, 1)
                dve.wait_ge(N.rstd, k * T + t + 1)
                for w in range(2):
                    c = slice(w * UNIT, (w + 1) * UNIT)
                    dve.wait_ge(dve_step, first + w)
                    stt(X[:, t, c], X[:, t, c], rstd[:, t:t + 1], lnw[:, 1, c], ALU.mult, ALU.add).then_inc(N.x_ready, 1)

            def ranks(v, n, out_):
                c1 = cg[:, 0:n * EG * EG].rearrange("p (g i j) -> p g i j", i=EG, j=EG)
                c2 = ch[:, 0:n * EG * EG].rearrange("p (g i j) -> p g i j", i=EG, j=EG)
                other, own = bc(v, 2, EG), bc(v, 3, EG)
                low = bc(const("lower").rearrange("p (i j) -> p i j", i=EG), 1, n)
                tt(c1, other, own, ALU.is_gt)
                step(tt(c2, other, own, ALU.is_ge))
                step(tt(c2, c2, low, ALU.mult))
                step(tt(c1, c1, c2, ALU.max))
                step(nc.vector.tensor_reduce(out_, c1, AX.X, ALU.add))

            def routing(C):
                dve.wait_ge(R.score, C.score + 1)
                dve.wait_ge(s_in, 112)
                step(tt(bs, sc, bc(rb, 1, T), ALU.add))
                b3 = bs.rearrange("p a (g e) -> p (a g) e", e=EG)
                r3 = rank[:, :].rearrange("p (g e) -> p g e", e=EG)
                s3 = sel2[:, :].rearrange("p (g e) -> p g e", e=EG)
                ranks(b3, T * EG, r3)
                step(ts(s3, r3, 1.5, None, ALU.is_lt))
                c3 = ch[:, 0:T * E].rearrange("p (g e) -> p g e", e=EG)
                step(tt(c3, b3, s3, ALU.mult))
                step(nc.vector.tensor_reduce(gs, c3, AX.X, ALU.add))
                ranks(gs[:, :].rearrange("p (a g) -> p a g", a=T), T, rank[:, 0:T * EG].rearrange("p (a g) -> p a g", a=T))
                step(ts(gsel, rank[:, 0:T * EG], 0.5, None, ALU.is_lt))
                f = sel.rearrange("p a (g e) -> p (a g) e", e=EG)
                tt(f, s3, bc(gsel, 2, EG), ALU.mult).then_inc(R.sel, 1)
                dve.wait_ge(R.sel, C.sel + 1)
                w = ch[:, 0:T * E].rearrange("p (a e) -> p a e", a=T)
                step(tt(w, sc, sel, ALU.mult))
                step(nc.vector.tensor_reduce(wsum, w, AX.X, ALU.add))
                step(nc.vector.reciprocal(wsum, wsum))
                dve.wait_ge(padded, 1)
                step(tt(gate[:, :, 0:E], w, bc(wsum, 2, E), ALU.mult))
                dve.wait_ge(R.pos, C.pos + 1)
                nc.vector.tensor_reduce(over[0:1, 0:1], ps[0:1, 1, 2 * E:3 * E], AX.X, ALU.max).then_inc(R.over, 1)
                step(nc.vector.scalar_tensor_tensor(pos[:, :, 0:E], ps[:, 1, 0:T * E].rearrange("p (a e) -> p a e", a=T), 1.0,
                                                    sel, ALU.add, ALU.mult))
                ts(pos[:, :, 0:E], pos[:, :, 0:E], -1.0, None, ALU.add).then_inc(R.table, 1)
                dve.wait_ge(R.table, C.table + 1)

            def one_hot(i):
                src = pos[:, :, bass.ds(2 * i, 2)] if not isinstance(i, int) else pos[:, :, 2 * i:2 * i + 2]
                return tt(Pm, bc(bc(const("slot"), 1, 2), 1, T), bc(src, 3, SLOTS), ALU.is_equal)

            def round_(rd, rho, shift):
                g0 = (PAIRS + 1) * rho
                if shift:
                    ts(pos, pos, float(-SLOTS), None, ALU.add).then_inc(rd.shift, 1)
                    dve.wait_ge(rd.shift, rho + 1)
                one_hot(0).then_inc(rd.onehot, 1)
                dve.wait_ge(rd.gathered, g0 + 1)
                copy(XeT[:, 4:8, :], ps[:, 3, :].rearrange("p (j c) -> p j c", j=4)).then_inc(rd.xe, 1)
                with dve.Fori(0, PAIRS) as i:
                    n, g = PAIRS * rho + i, g0 + i
                    dve.wait_ge(rd.gp, g + 1)
                    dve.wait_ge(rd.gathered, g + 1)
                    one_hot(i + 1).then_inc(rd.onehot, 1)
                    dve.wait_ge(rd.silu, n + 1)
                    dve.wait_ge(rd.up_done, n + 1)
                    tt(hid, sg, ps[:, 1, :], ALU.mult).then_inc(rd.h, 1)
                    dve.wait_ge(rd.gathered, g + 2)
                    copy(XeT[:, 4:8, :], ps[:, 3, :].rearrange("p (j c) -> p j c", j=4)).then_inc(rd.xe, 1)
                    dve.wait_ge(rd.ht, n + 1)
                    copy(hT, ps[:, 0, :].rearrange("p (k c) -> p k c", k=FJ)).then_inc(rd.ht_sb, 1)
                    dve.wait_ge(rd.y, 2 * n + 1)
                    copy(Y[:, 0:UNIT], ps[:, 2, :]).then_inc(rd.y_d, 1)
                dve.wait_ge(rd.comb, T * PAIRS * (rho + 1))
                dve.wait_ge(rd.gp, g0 + PAIRS + 1)
                dve.sem_inc(round_over, 1)

            dve.wait_ge(c_in, 16)
            copy(identb[:, :], ident).then_inc(bconst, 1)
            copy(causalb[:, :], const("causal")).then_inc(bconst, 1)
            copy(cmaskb[:, :, :, :], const("cmask").rearrange("p (t g k) -> p t g k", t=T, g=G)).then_inc(bconst, 1)
            for l in range(2):
                B, C = base[l], rbase[l]
                for a in range(T):
                    transposed(xT, a, L.xt, B.xt, L.xt_sb)
                for r in range(2):
                    rope(l, r)
                if l == 0:
                    dve.wait_ge(s_in, 112)
                    for w in range(2):
                        for gp in range(2):
                            dve.wait_ge(kcvc_t, 2 * w + gp + 1)
                            for par in range(2):
                                h = slice(64 * par, 64 * par + 64)
                                src = ps[h, 4 + 2 * w + gp, :].rearrange("p (g n m) -> p g n m", g=2, m=2 * 8)
                                last = None
                                for half_ in range(2):
                                    s4 = src[:, :, half_:half_ + NC, par:16:2]
                                    d4 = stat_kv[w][h, 8 * half_:8 * half_ + 8, 2 * gp:2 * gp + 2, :].rearrange("p m g n -> p g n m")
                                    pp = bc(bc(posT[h, w, 8 * half_:8 * half_ + 8], 1, NC), 1, 2)
                                    last = tt(d4, s4, pp, ALU.add)
                                last.then_inc(stat_done, 1)
                for r in range(2, 6):
                    rope(l, r)
                if l == 0:
                    dve.wait_ge(w2_done, 1)
                    n = G * NC
                    rope_mul(ps[0:n, 6, 0:DH], kca[0:n, :], kcb[0:n, :], const("ccos")[0:n, :], const("csin")[0:n, :]
                             ).then_inc(kc_rope, 1)
                    dve.wait_ge(padded, 1)
                    copy(vc[0:n, :], ps[0:n, 6, DH:2 * DH])
                    copy(vc[64:64 + n, :], ps[0:n, 6, DH:2 * DH]).then_inc(vc_done, 1)
                for r in range(6, 8):
                    rope(l, r)
                if l == 0:
                    dve.wait_ge(L.copied, 7)
                    for t in range(T):
                        last = ts(gates[:, t, 0:H], gates[:, t, 0:H], const("valid")[:, t:t + 1], None, ALU.mult)
                    step(last)
                n, nb = len(ITEMS[l]), BRANCHES[l]
                for m in range(n + 4):
                    if m < n:
                        attention_max(l, m)
                    if 1 <= m <= n:
                        coefficients(l, m - 1)
                    if 2 <= m < n + 2:
                        dve.wait_ge(L.pt, B.pt + m - 1)
                        w = 384 if ITEMS[l][m - 2][1] else P
                        copy(PTb[m % 2][:, 0, 0:w], ps[:, 4, 0:w]).then_inc(L.pt_sb, 1)
                    if m >= 4 and (m - 4) % nb == nb - 1:
                        dve.wait_ge(L.pv, B.pv + m - 3)
                        jq = (m - 4) // nb
                        copy(OT[:, jq, :], ps[:, 6 + jq % 2, 0:S]).then_inc(L.ot_sb, 1)
                for t in range(T):
                    layer_norm(2 * l, t, L.mix, [B.mix + 2 * t + 1, B.mix + 2 * t + 2], L.ln_in, B.ln_in + 32)
                    transposed(xTr, t, R.xt, C.xt, R.xt_sb)
                routing(C)
                round_(main, l, False)
                most = dve.value_load(over[0:1, 0:1], min_val=0, max_val=S)
                with dve.If(most > SLOTS):
                    with dve.Fori(0, ROUNDS - 1) as rho:
                        round_(rounds[1 + l], rho, True)
                for t in range(T):
                    layer_norm(2 * l + 1, t, main.comb, [T * (PAIRS * (l + 1) - 1) + t + 1] * 2, R.ln_in, C.ln_in + 32)


def kernel(**inputs):
    import concourse.bacc as bacc
    from concourse.bass_utils import run_bass_kernel_spmd

    a = {k: np.asarray(v) for k, v in inputs.items()}
    places = lambda p: np.ascontiguousarray(p[0].reshape(CL // 2, 2 * DH).T)
    beside = lambda w: w.reshape(2, 2, 4, DH, D).transpose(0, 2, 1, 3, 4).reshape(D, D)
    arrays = {
        "x": a["x"][0], "consts": constants(), "w_in0": a["nsa_w_in"][0], "w_out0": beside(a["nsa_w_out"][0]),
        "cmp_kw1": a["nsa_cmp_k_w1"][0], "cmp_kw2": a["nsa_cmp_k_w2"][0],
        "cmp_vw1": a["nsa_cmp_v_w1"][0], "cmp_vw2": a["nsa_cmp_v_w2"][0],
        "cmp_kpos": places(a["nsa_cmp_k_pos"]), "cmp_vpos": places(a["nsa_cmp_v_pos"]),
        "w_in1": a["moba_w_in"][0], "w_out1": a["moba_w_out"][0],
        "router_w": a["router_w"], "router_b": a["router_bias"].reshape(1, E),
        "w_gate": a["moe_w_gate"], "w_up": a["moe_w_up"], "w_down": a["moe_w_down"],
        "ln_g": a["ln_g"], "ln_b": a["ln_b"],
    }
    nc = bacc.Bacc("TRN2", target_bir_lowering=False, num_devices=1)
    feed, args = {}, []
    for name, v in arrays.items():
        v = np.ascontiguousarray(v)
        feed[f"in_{name}"] = v
        args.append(nc.dram_tensor(f"in_{name}", v.shape, mybir.dt.from_np(v.dtype), kind="ExternalInput").ap())
    args.append(nc.dram_tensor("out", (S, D), F32, kind="ExternalOutput").ap())
    build(nc, *args)
    r = run_bass_kernel_spmd(nc, [feed], core_ids=[0])
    return r.results[0]["out"].reshape(1, S, D)
```

```python
from collections import namedtuple
from contextlib import ExitStack

import numpy as np
import concourse.bass as bass
from concourse import mybir

F32 = mybir.dt.float32
F32R = mybir.dt.float32r
BF16 = mybir.dt.bfloat16
I32 = mybir.dt.int32
ALU = mybir.AluOpType
ACT = mybir.ActivationFunctionType
AX = mybir.AxisListType

P = 128
D, S = 1024, 256
T = S // P
KJ = D // P
H, DH = 16, 64
G, HPG = 4, 4
UNIT = 512
NEG = -1e30
ALPHA = 4.0 ** 0.25
EPS = 1e-5
CL, CS = 32, 16
NC = (S - CL) // CS + 1
CH = 256
E, EG = 16, 4
FE = 512
FJ = FE // P
PAIRS = E // 2
SLOTS = 64
ROUNDS = S // SLOTS
WBUF = 3
RING = 6

CONST = {}
_at = 0
for _name, _n in (("ident", P), ("alphai", P), ("causal", P), ("before", P), ("ones", P),
                  ("cosq", T * DH), ("sinq", T * DH), ("cosk", T * DH), ("sink", T * DH),
                  ("ccos", DH), ("csin", DH), ("slot", SLOTS), ("lower", EG * EG), ("valid", T), ("cmask", T * G * DH)):
    CONST[_name] = (_at, _n)
    _at += _n
NCONST = _at
NKEPT = NCONST - CONST["cmask"][1]


def constants():
    c = np.zeros((P, NCONST), np.float32)

    def put(name, a):
        at, n = CONST[name]
        c[:a.shape[0], at:at + n] = a.reshape(a.shape[0], n)

    p = np.arange(P)
    put("ident", np.eye(P))
    put("alphai", np.eye(P) * ALPHA)
    put("causal", np.where(p[None, :] > p[:, None], NEG, 0.0))
    put("before", (p[:, None] < p[None, :]) * 1.0)
    put("ones", np.ones((P, P)))
    f = np.float32
    inv = f(1.0) / (f(10000.0) ** (np.arange(0, DH, 2, dtype=f) / f(DH)))

    def rope(pos):
        ang = pos.astype(f)[:, None] * inv[None, :]
        cos, sin = np.cos(ang), np.sin(ang)
        return np.concatenate([cos, cos], 1), np.concatenate([-sin, sin], 1)

    cos, sin = rope(np.arange(S))
    tiles = lambda a: a.reshape(T, P, -1).transpose(1, 0, 2)
    put("cosk", tiles(cos))
    put("sink", tiles(sin))
    put("cosq", tiles(cos * f(DH ** -0.5)))
    put("sinq", tiles(sin * f(DH ** -0.5)))
    end = np.arange(NC) * CS + CL - 1
    cos, sin = rope(end)
    put("ccos", np.tile(cos, (G, 1)))
    put("csin", np.tile(sin, (G, 1)))
    m = np.full((S, G, DH), NEG, f)
    for g in range(G):
        m[:, g, g * NC:(g + 1) * NC] = np.where(end[None, :] <= np.arange(S)[:, None], 0.0, NEG)
    put("cmask", tiles(m.reshape(S, G * DH)))
    put("valid", tiles((np.arange(S) >= CL - 1)[:, None] * 1.0))
    put("slot", np.broadcast_to(np.arange(SLOTS), (P, SLOTS)))
    put("lower", np.broadcast_to((np.arange(EG)[None, :] < np.arange(EG)[:, None]) * 1.0, (P, EG, EG)))
    return c


def build(nc, x, consts, w_in0, w_out0, cmp_kw1, cmp_kw2, cmp_vw1, cmp_vw2, cmp_kpos, cmp_vpos,
          w_in1, w_out1, router_w, router_b, w_gate, w_up, w_down, ln_g, ln_b, out):
    ctx = ExitStack()
    with ctx:
        def sb(name, shape, dt=F32):
            return ctx.enter_context(nc.sbuf_tensor(name, shape, dt))

        def sem(name):
            return ctx.enter_context(nc.semaphore(name))

        ring = sb("ring", [P, RING, KJ * UNIT])
        area = sb("area", [P, 2, KJ // 2, UNIT])
        wh = sb("wh", [P, WBUF, UNIT], F32R)
        wl = sb("wl", [P, WBUF, UNIT], F32R)
        cst = sb("cst", [P, NKEPT])
        X = sb("X", [P, T, D])
        xh = sb("xh", [P, KJ, S], F32R)
        xl = sb("xl", [P, KJ, S], F32R)
        R2 = sb("R2", [P, T * D])
        R3 = sb("R3", [P, T * D])
        R4 = sb("R4", [P, T * D])
        R5 = sb("R5", [P, 3 * D])
        R6 = sb("R6", [P, 3 * D])
        small = sb("small", [P, 1024])
        rw = sb("rw", [P, KJ, E])
        identb = sb("identb", [P, P], BF16)
        causalb = sb("causalb", [P, P], BF16)
        cmaskb = sb("cmaskb", [P, T, G, DH], BF16)
        over = sb("over", [1, 2], I32)
        ps = ctx.enter_context(nc.psum_tensor("ps", [P, 8, 512], F32))

        def const(name):
            at, n = CONST[name]
            return cst[:, at:at + n]

        ident = const("ident")
        used = [0]

        def tiny(n):
            used[0] += n
            assert used[0] <= 1024
            return small[:, used[0] - n:used[0]]

        qT = R2[:, :].rearrange("p (j t) -> p j t", j=KJ)
        OT = [R6[:, 1536 + j * S:1536 + (j + 1) * S] for j in range(6)] + [R5[:, 2304 + j * S:2304 + (j + 1) * S] for j in range(2)]
        xTr = R3[:, :].rearrange("p (j t) -> p j t", j=KJ)
        Xp = R2[:, :].rearrange("p (a j c) -> p a j c", a=T, j=KJ)
        XeT = R3[:, 0:KJ * P].rearrange("p (j c) -> p j c", j=KJ)
        Y = R3[:, D:2 * D]
        stage = [R6[:, n * UNIT:(n + 1) * UNIT] for n in range(2)]
        rope_b = [R6[:, (2 + n) * UNIT:(3 + n) * UNIT] for n in range(2)]
        Pb = [R5[:, n * 768:(n + 1) * 768] for n in range(3)]
        PTb = [R6[:, n * 768:(n + 1) * 768].rearrange("p (a k) -> p a k", a=2) for n in range(2)]
        wgt = R5[:, 1920:2304].rearrange("p (j c) -> p j c", j=KJ)
        cmask = R3[:, 0:T * G * DH]
        lnw = R5[:, 0:2 * D].rearrange("p (w c) -> p w c", w=2)
        stat_kv = [R5[:, n * 960:(n + 1) * 960].rearrange("p (m g n) -> p m g n", m=CL // 2, g=G) for n in range(2)]
        raw = R2[:, :].rearrange("p (a g u c) -> p a g u c", a=T, g=2 * G, u=2)
        hg = R4[:, D:D + CH]
        hgT = R4[:, D + 256:D + 512].rearrange("p (k c) -> p k c", k=2)
        w2 = R4[:, D + 512:D + 768].rearrange("p (w k c) -> p w k c", w=2, k=2)
        kcT = R4[:, D + 768:D + 832]
        vc = R4[:, D + 832:D + 896]
        kca = R3[:, D:D + 64]
        kcb = R3[:, D + 64:D + 128]
        kcr = R3[:, D + 128:D + 256]
        hid = R4[:, 0:FE]
        sg = R4[:, FE:2 * FE]
        hT = R4[:, 2 * FE:3 * FE].rearrange("p (k c) -> p k c", k=FJ)
        Pm = R4[:, 1536:1792].rearrange("p (a e c) -> p a e c", a=T, e=2)
        GP = R4[:, 1792:2048].rearrange("p (a e c) -> p a e c", a=T, e=2)
        GT = R6[:, 0:256].rearrange("p (a c) -> p a c", a=T)

        gates = tiny(T * 3 * H).rearrange("p (a h) -> p a h", a=T)
        posT = tiny(2 * 16).rearrange("p (w m) -> p w m", w=2)
        sums = tiny(12).rearrange("p (b t a) -> p b t a", b=3, t=T)
        nmax = tiny(8).rearrange("p (b a h) -> p b a h", b=2, a=T)
        coef = tiny(12).rearrange("p (b t a) -> p b t a", b=3, t=T)
        bst = tiny(T * 12).rearrange("p (a h s) -> p a h s", a=T, h=2)
        mv = tiny(T * 2).rearrange("p (a s) -> p a s", a=T)
        ve = tiny(T)
        half = tiny(T)
        rstd = tiny(T)
        rb = tiny(E)
        sc = tiny(T * E).rearrange("p (a e) -> p a e", a=T)
        bs = tiny(T * E).rearrange("p (a e) -> p a e", a=T)
        cg = tiny(T * E * EG)
        ch = tiny(T * E * EG)
        rank = tiny(T * E)
        sel2 = tiny(T * E)
        gs = tiny(T * EG)
        gsel = tiny(T * EG)
        sel = tiny(T * E).rearrange("p (a e) -> p a e", a=T)
        wsum = tiny(T)
        EP = E + 2
        pos = tiny(T * EP).rearrange("p (a e) -> p a e", a=T)
        gate = tiny(T * EP).rearrange("p (a e) -> p a e", a=T)

        x_in, ident_in, c_in, s_in = sem("x_in"), sem("ident_in"), sem("c_in"), sem("s_in")
        cmpw_in = sem("cmpw_in")
        area_in = [sem("area_in0"), sem("area_in1")]
        out_used = sem("out_used")
        w_hi, w_lo, w_used = sem("w_hi"), sem("w_lo"), sem("w_used")
        cmpw_used = sem("cmpw_used")
        bconst = sem("bconst")
        out_done = sem("out_done")
        padded, round_over = sem("padded"), sem("round_over")
        dve_step, pool_step = sem("dve_step"), sem("pool_step")
        LS = namedtuple("LS", "xt xh xt_sb proj rope_mul roped copied tr tr_copied s_done mx exp coef scaled "
                              "pt pt_sb pv ot_sb mix ln_in")
        L = LS(*(sem(n) for n in LS._fields))
        base = [LS(*[0] * len(LS._fields)),
                LS(xt=4, xh=4, xt_sb=4, proj=11, rope_mul=8, roped=8, copied=7, tr=8, tr_copied=8, s_done=24, mx=24, exp=24,
                   coef=24, scaled=24, pt=24, pt_sb=48, pv=24, ot_sb=8, mix=4, ln_in=32)]
        kcvc_t, stat_done, gelu, hg_t, hgt_sb, w2_done, kc_rope, kc_add, vc_done, kct, kct_sb, hg_zero = (
            sem(n) for n in "kcvc_t stat_done gelu hg_t hgt_sb w2_done kc_rope kc_add vc_done kct kct_sb hg_zero".split())
        LN = namedtuple("LN", "stats rstd x_ready")
        N = LN(*(sem(f"ln_{n}") for n in LN._fields))

        def ready(k, t, w):
            return 2 * (k * T + t) + w + 1

        RT = namedtuple("RT", "xt xt_sb logits score sel pos table over xp ln_in")
        R = RT(*(sem(f"route_{n}") for n in RT._fields))
        rbase = [RT(*[0] * len(RT._fields)), RT(4, 4, 1, 1, 1, 1, 1, 1, T, 32)]
        RD = namedtuple("RD", "w gate_half gate_done up_done gathered onehot gp silu h xe gt gt_copied ht ht_sb "
                              "y y_d y_a comb shift")
        rounds = [RD([sem(f"w{s}_{k}") for s in range(4)], *(sem(f"{n}_{k}") for n in RD._fields[1:]))
                  for k in ("main", "more0", "more1")]
        main = rounds[0]

        NSA_COLS = [1024, 1536, 2048, 0, 512]
        ROPE0 = [2, 0]
        ROPED = [8, 8]
        LAST = [11, 12]
        AREA0 = [0, 7]
        OUT = [5, 6, 13, 14]

        GATES = 5 * KJ
        chunk = lambda u, j: u * KJ + j if u < 5 else GATES + 1 + (u - 7) * KJ + j

        def wait_buffer(eng, c):
            c -= WBUF
            if c < 0:
                return
            if c == GATES:
                eng.wait_ge(L.proj, 11)
                return
            l, v, j = (0, c // KJ, c % KJ) if c < GATES else (1, (c - GATES - 1) // KJ, (c - GATES - 1) % KJ)
            if j == KJ - 1:
                eng.wait_ge(L.proj, base[l].proj + 2 * (v + 1))
            else:
                eng.wait_ge(w_used, (5 * l + v) * (KJ - 1) + j + 1)

        def ropes(l, n):
            return max(0, min(n + 1 - ROPE0[l], ROPED[l]))

        def copies(l, n):
            return min(n + 1, 6) + (n >= 10) if l == 0 else max(0, n + 1 - 8)

        ITEMS = [[(jq, br, 2 * (br - 1) + jq // 4, [256 * (br - 1) + 64 * (2 * (jq // 4) + a) for a in range(2)])
                  for jq in range(H // 2) for br in (1, 2, 0)],
                 [(j, 1, j, [128 * j + 64 * a for a in range(2)]) for j in range(H // 2)]]
        BRANCHES = [3, 1]

        block = ctx.enter_context(nc.Block())

        @block.sync
        def _(sp):
            def unit_src(u):
                if u < 5:
                    return w_in0[:, NSA_COLS[u]:NSA_COLS[u] + UNIT]
                if u < 7:
                    return w_out0[:, (u - 5) * UNIT:(u - 4) * UNIT]
                if u < 13:
                    return w_in1[:, (u - 7) * UNIT:(u - 6) * UNIT]
                return w_out1[:, (u - 13) * UNIT:(u - 12) * UNIT]

            def load_unit(u):
                for h in range(2):
                    v = u - 1
                    if v in OUT:
                        if h == 0:
                            sp.wait_ge(out_used, OUT.index(v) + 1)
                        else:
                            l, w = divmod(OUT.index(v), 2)
                            sp.wait_ge(L.mix, base[l].mix + 2 * w + 2)
                    elif v >= 0:
                        sp.wait_ge(w_lo, chunk(v, 4 * h + 3) + 1)
                    sp.dma_start(area[:, h], unit_src(u).rearrange("(j p) n -> p j n", p=P)[:, 4 * h:4 * h + 4]
                                 ).then_inc(area_in[h], 16)

            def load_slot(rd, l, experts, s, halves=(0, 1)):
                if s < 4:
                    i = experts[s % 2]
                    src = (w_gate, w_up)[s // 2][l, bass.ds(i, 1) if not isinstance(i, int) else slice(i, i + 1)]
                    src = src.rearrange("a (p j) n -> p (a j n)", p=P)
                    if s < 2:
                        for h in halves:
                            c = slice(h * KJ // 2 * UNIT, (h + 1) * KJ // 2 * UNIT)
                            sp.dma_start(ring[:, s, c], src[:, c]).then_inc(rd.w[0], 16)
                    else:
                        sp.dma_start(ring[:, s], src).then_inc(rd.w[1], 16)
                else:
                    i, c = experts[0], slice((s - 4) * UNIT, (s - 3) * UNIT)
                    src = w_down[l, bass.ds(i, 2) if not isinstance(i, int) else slice(i, i + 2)][:, :, c]
                    sp.dma_start(ring[:, s].rearrange("p (k n) -> p k n", k=2 * FJ),
                                 src.rearrange("a (k p) n -> p (a k) n", p=P)).then_inc(rd.w[s - 2], 16)

            def load_ln(k, signal):
                l, s = k // 2, k % 2
                sp.dma_start(lnw[:, 0], ln_g[l, s:s + 1].to_broadcast([P, D])).then_inc(signal, 16)
                sp.dma_start(lnw[:, 1], ln_b[l, s:s + 1].to_broadcast([P, D])).then_inc(signal, 16)

            def rest_of_round(rd, l, rho):
                with sp.Fori(1, PAIRS) as i:
                    n, n2 = sp.snap(i + PAIRS * rho), sp.snap(2 * i + 2 * PAIRS * rho)
                    n1 = sp.snap(2 * i + (2 * PAIRS * rho - 1))
                    experts = [sp.snap(2 * i), sp.snap(2 * i + 1)]
                    for h, used in ((0, rd.gate_half), (1, rd.gate_done)):
                        sp.wait_ge(used, n)
                        for s in range(2):
                            load_slot(rd, l, experts, s, (h,))
                    for s in range(2, RING):
                        if s < 4:
                            sp.wait_ge(rd.up_done, n)
                        else:
                            sp.wait_ge(rd.y, n2 if s == 5 else n1)
                        load_slot(rd, l, experts, s)

            sp.dma_start(X[:, :, :], x.rearrange("(a p) c -> p a c", p=P)).then_inc(x_in, 16)
            sp.dma_start(cst[:, 0:P], consts[:, 0:P]).then_inc(ident_in, 16)
            load_unit(0)
            sp.dma_start(cst[:, P:], consts[:, P:NKEPT]).then_inc(c_in, 16)
            sp.dma_start(cmask, consts[:, NKEPT:]).then_inc(c_in, 16)
            for s, (w2_, pos_) in enumerate(((cmp_kw2, cmp_kpos), (cmp_vw2, cmp_vpos))):
                sp.dma_start(w2[:, s], w2_.rearrange("(k p) n -> p k n", p=P)).then_inc(s_in, 16)
                sp.dma_start(posT[:, s], pos_).then_inc(s_in, 16)
            sp.dma_start(wgt[:, :, :], w_in0[:, 2560:2608].rearrange("(j p) n -> p j n", p=P)).then_inc(s_in, 16)
            sp.dma_start(rw[:, :, :], router_w.rearrange("(j p) n -> p j n", p=P)).then_inc(s_in, 16)
            sp.dma_start(rb, router_b.to_broadcast([P, E])).then_inc(s_in, 16)
            load_unit(1)
            load_unit(2)
            for s, w in ((4, cmp_kw1), (5, cmp_vw1)):
                sp.dma_start(ring[:, s].rearrange("p (m n) -> p m n", m=CL // 2),
                             w.rearrange("(m p) n -> p m n", p=P)).then_inc(cmpw_in, 16)
                load_unit(s - 1)
            for s in range(4):
                load_slot(main, 0, (0, 1), s)
            load_unit(5)
            sp.wait_ge(cmpw_used, 1)
            load_slot(main, 0, (0, 1), 4)
            load_slot(main, 0, (0, 1), 5)
            for l in range(2):
                B, C, extra = base[l], rbase[l], rounds[1 + l]
                sp.wait_ge(L.pt, B.pt + len(ITEMS[l]))
                load_ln(2 * l, L.ln_in)
                if l == 0:
                    load_unit(6)
                    load_unit(7)
                else:
                    load_unit(14)
                sp.wait_ge(N.x_ready, ready(2 * l, T - 1, 1))
                load_ln(2 * l + 1, R.ln_in)
                rest_of_round(main, l, l)
                sp.wait_ge(R.over, C.over + 1)
                most = sp.value_load(over[0:1, 0:1], min_val=0, max_val=S)
                with sp.If(most > SLOTS):
                    sp.wait_ge(main.comb, T * PAIRS * (l + 1))
                    with sp.Fori(0, ROUNDS - 1) as rho:
                        for s in range(RING):
                            load_slot(extra, l, (0, 1), s)
                        rest_of_round(extra, l, rho)
                        sp.wait_ge(extra.comb, T * PAIRS * (rho + 1))
                        sp.sem_inc(round_over, 1)
                if l == 0:
                    for s in range(RING):
                        sp.wait_ge(main.gate_done if s < 2 else main.up_done if s < 4 else main.y,
                                   PAIRS if s < 4 else 2 * PAIRS - (s == 4))
                        load_slot(main, 1, (0, 1), s)
                        if s >= 3:
                            load_unit(2 * s + 2)
                            load_unit(2 * s + 3)
            for a in range(T):
                sp.wait_ge(N.x_ready, ready(3, a, 1))
                sp.dma_start(out[a * P:(a + 1) * P, :], X[:, a]).then_inc(out_done, 16)
            sp.wait_ge(out_done, 16 * T)

        def bc(ap, axis, n):
            ap = ap.unsqueeze(axis)
            shape = list(ap.shape)
            shape[axis] = n
            return ap.to_broadcast(shape)

        V = [R4[:, 0:D].rearrange("p (a c) -> p a c", a=T), R4[:, :].rearrange("p (a c) -> p a c", a=T)]
        kT = R3[:, :].rearrange("p (j t) -> p j t", t=S)
        AREA_IN = lambda u, h: (area_in[h], 16 * (u + 1))

        @block.tensor
        def _(pe):
            mm, tp = nc.tensor.matmul, nc.tensor.transpose

            def transpose_tile(a, signal, wait):
                for w in range(2):
                    wait(w)
                    for jj in range(4):
                        j = 4 * w + jj
                        last = tp(ps[:, 2 * a + w, jj * P:(jj + 1) * P], X[:, a, j * P:(j + 1) * P], ident)
                    last.then_inc(signal, 1)

            def project(l, i):
                B = base[l]
                n = 2 * i
                if n >= 4:
                    if ropes(l, n - 3):
                        pe.wait_ge(L.rope_mul, B.rope_mul + ropes(l, n - 3))
                    if copies(l, n - 3):
                        pe.wait_ge(L.copied, B.copied + copies(l, n - 3))
                for j in range(KJ):
                    c = chunk(AREA0[l] + i, j)
                    pe.wait_ge(w_lo, c + 1)
                    for a in range(T):
                        to, tok = ps[:, (n + a) % 4, :], slice(a * P, (a + 1) * P)
                        mm(to, xh[:, j, tok], wh[:, c % WBUF], start=(j == 0), stop=False)
                        mm(to, xh[:, j, tok], wl[:, c % WBUF], start=False, stop=False)
                        last = mm(to, xl[:, j, tok], wh[:, c % WBUF], start=False, stop=(j == KJ - 1))
                        if j == KJ - 1:
                            last.then_inc(L.proj, 1)
                    if j < KJ - 1:
                        last.then_inc(w_used, 1)

            def transpose_roped(l, r):
                B = base[l]
                pe.wait_ge(L.roped, B.roped + r + 1)
                if r >= 2:
                    pe.wait_ge(L.tr_copied, B.tr_copied + r - 1)
                elif l == 0:
                    pe.wait_ge(stat_done, 4)
                narrow = l == 0 and r < 4
                for b in range(2 if narrow else 4):
                    st = stage[r % 2]
                    last = tp(ps[:, 4 + r % 2, b * P:(b + 1) * P], st[:, b * P:(b + 1) * P], ident)
                last.then_inc(L.tr, 1)

            def scores(l, m):
                B = base[l]
                jq, br, jk, _ = ITEMS[l][m]
                if m == 0:
                    pe.wait_ge(L.tr_copied, B.tr_copied + 8)
                    pe.wait_ge(L.copied, B.copied + copies(l, LAST[l] - 1))
                    pe.wait_ge(bconst, 3)
                if m >= 2:
                    pe.wait_ge(L.exp, B.exp + m - 1)
                half_ = [slice(64 * a, 64 * a + 64) for a in range(2)]
                banks = [2 * (m % 2) + a for a in range(2)]
                for t in range(T):
                    at, n = (t * P, (t + 1) * P) if br else (t * DH, DH)
                    for a in range(2):
                        mm(ps[:, banks[a], at:at + n], qT[half_[a], jq, t * P:(t + 1) * P],
                           kT[half_[a], jk, 0:n] if br else kcT[half_[a], :], start=True, stop=False)
                    for a in range(2):
                        if br:
                            last = mm(ps[:, banks[a], at + t * P:at + n], identb[:, :], causalb[:, :], start=False, stop=True)
                        else:
                            last = mm(ps[:, banks[a], at:at + n], identb[:, :], cmaskb[:, t, 2 * (jq // 4) + a, :],
                                      start=False, stop=True)
                last.then_inc(L.s_done, 1)

            def transpose_probs(l, m):
                B = base[l]
                pe.wait_ge(L.scaled, B.scaled + m + 1)
                if m >= 1:
                    pe.wait_ge(L.pt_sb, B.pt_sb + 2 * m)
                if ITEMS[l][m][1]:
                    for a in range(2):
                        for b in range(3):
                            at = 384 * a + b * P
                            last = tp(ps[:, 4 + a, b * P:(b + 1) * P], Pb[m % 3][:, at:at + P], ident)
                else:
                    for t in range(T):
                        last = tp(ps[:, 4 + t, 0:P], Pb[m % 3][:, t * P:(t + 1) * P], ident)
                last.then_inc(L.pt, 1)

            def times_v(l, m):
                B = base[l]
                jq, br, _, cols = ITEMS[l][m]
                nb = BRANCHES[l]
                pe.wait_ge(L.pt_sb, B.pt_sb + 2 * m + 2)
                if m % nb == 0 and jq >= 2:
                    pe.wait_ge(L.ot_sb, B.ot_sb + jq - 1)
                if m == 0 and l == 0:
                    pe.wait_ge(kct_sb, 1)
                    pe.wait_ge(vc_done, 1)
                    pe.wait_ge(kc_rope, 1)
                first, end = m % nb == 0, m % nb == nb - 1
                o = ps[:, 6 + jq % 2, 0:S]
                pt = PTb[m % 2]
                if br:
                    for a in range(2):
                        last = mm(o[64 * a:64 * a + 64, :], V[l][:, 0, cols[a]:cols[a] + DH], pt[:, a, 0:2 * P],
                                  start=first, stop=False, skip_group_check=True)
                    for a in range(2):
                        last = mm(o[64 * a:64 * a + 64, P:2 * P], V[l][:, 1, cols[a]:cols[a] + DH], pt[:, a, 2 * P:3 * P],
                                  start=False, stop=end, skip_group_check=True)
                else:
                    for a in range(2):
                        h = slice(64 * a, 64 * a + 64)
                        last = mm(o[h, :].rearrange("p (t c) -> p t c", t=T), vc[h, :], pt[h, :, 0:P],
                                  start=False, stop=end, skip_group_check=True)
                last.then_inc(L.pv, 1)

            def attention(l):
                n = len(ITEMS[l])
                for m in range(n + 3):
                    if m < n:
                        scores(l, m)
                    if 2 <= m < n + 2:
                        transpose_probs(l, m - 2)
                    if m >= 3:
                        times_v(l, m - 3)

            def mix_out(l):
                B = base[l]
                for a in range(T):
                    if a:
                        pe.wait_ge(L.ot_sb, B.ot_sb + H // 2)
                    for w in range(2):
                        seed(a, w, False)
                for w, parts in ((0, ((0, 0), (0, 1), (1, 0), (1, 1))), (1, ((0, 0), (1, 0), (0, 1), (1, 1)))):
                    u = OUT[2 * l + w]
                    for n, (h, a) in enumerate(parts):
                        pe.wait_ge(*AREA_IN(u, h))
                        for j in range(4 * h, 4 * h + 4):
                            last = mm(ps[:, 4 + 2 * a + w, :], OT[j][:, a * P:(a + 1) * P], area[:, h, j % 4, :],
                                      start=False, stop=(j == KJ - 1), skip_group_check=True)
                        if h:
                            last.then_inc(L.mix, 1)
                        elif a:
                            last.then_inc(out_used, 1)

            def seed(a, w, stop):
                mm(ps[:, 4 + 2 * a + w, :], const("alphai"), X[:, a, w * UNIT:(w + 1) * UNIT],
                   start=True, stop=stop, skip_group_check=True)

            def logits(l, a):
                pe.wait_ge(R.xt_sb, rbase[l].xt_sb + 2 * a + 2)
                for j in range(KJ):
                    last = mm(ps[:, 0, a * E:(a + 1) * E], xTr[:, j, a * P:(a + 1) * P], rw[:, j, :],
                              start=(j == 0), stop=(j == KJ - 1))
                return last

            def gather(rd):
                for j in range(KJ):
                    for a in range(T):
                        last = mm(ps[:, 2 + j // 4, (j % 4) * P:(j % 4 + 1) * P], Xp[:, a, j, :],
                                  Pm[:, a].rearrange("p e c -> p (e c)"), start=(a == 0), stop=(a == T - 1))
                last.then_inc(rd.gathered, 1)

            def round_(rd, rho):
                pe.wait_ge(rd.onehot, (PAIRS + 1) * rho + 1)
                gather(rd)
                with pe.Fori(0, PAIRS) as i:
                    n, g = PAIRS * rho + i, (PAIRS + 1) * rho + i
                    pe.wait_ge(rd.xe, 2 * g + 2)
                    for w, done in ((0, rd.gate_done), (1, rd.up_done)):
                        pe.wait_ge(rd.w[w], (64, 32)[w] * (n + 1))
                        for j in range(KJ):
                            for e in range(2):
                                last = mm(ps[64 * e:64 * e + 64, w, :], XeT[:, j, 64 * e:64 * e + 64],
                                          ring[:, 2 * w + e, j * UNIT:(j + 1) * UNIT], start=(j == 0), stop=(j == KJ - 1))
                            if w == 0 and j == KJ // 2 - 1:
                                last.then_inc(rd.gate_half, 1)
                        last.then_inc(done, 1)
                    pe.wait_ge(rd.onehot, g + 2)
                    gather(rd)
                    pe.wait_ge(rd.gp, g + 1)
                    pe.wait_ge(rd.h, n + 1)
                    for a in range(T):
                        last = tp(ps[:, 1, a * P:(a + 1) * P], GP[:, a].rearrange("p e c -> p (e c)"), ident)
                    last.then_inc(rd.gt, 1)
                    for k in range(FJ):
                        last = tp(ps[:, 0, k * P:(k + 1) * P], hid[:, k * P:(k + 1) * P], ident)
                    last.then_inc(rd.ht, 1)
                    pe.wait_ge(rd.xe, 2 * g + 4)
                    pe.wait_ge(rd.ht_sb, n + 1)
                    for w in range(2):
                        pe.wait_ge(rd.w[2 + w], 16 * n + 16)
                        for k in range(FJ):
                            for e in range(2):
                                last = mm(ps[64 * e:64 * e + 64, 2 + w, :], hT[:, k, 64 * e:64 * e + 64],
                                          ring[:, 4 + w, (e * FJ + k) * UNIT:(e * FJ + k + 1) * UNIT],
                                          start=(k == 0), stop=(k == FJ - 1))
                        last.then_inc(rd.y, 1)
                    pe.wait_ge(rd.gt_copied, n + 1)
                    pe.wait_ge(rd.y_d, n + 1)
                    pe.wait_ge(rd.y_a, n + 1)
                    for a in range(T):
                        for w in range(2):
                            last = mm(ps[:, 4 + 2 * a + w, :], GT[:, a, :], Y[:, w * UNIT:(w + 1) * UNIT],
                                      start=False, stop=True, skip_group_check=True)
                        last.then_inc(rd.comb, 1)

            pe.wait_ge(ident_in, 16)
            for l in range(2):
                B, C = base[l], rbase[l]
                for a in range(T):
                    transpose_tile(a, L.xt, (lambda w: pe.wait_ge(x_in, 16)) if l == 0 else
                                   (lambda w: pe.wait_ge(N.x_ready, ready(1, a, w))))
                pe.wait_ge(L.xt_sb, B.xt_sb + 4)
                project(l, 0)
                project(l, 1)
                if l == 0:
                    pe.wait_ge(L.copied, B.copied + 2)
                    for w in range(2):
                        for g in range(G):
                            for a in range(T):
                                blk = raw[:, a, G * w + g].rearrange("p u c -> p (u c)")
                                last = tp(ps[:, 4 + 2 * w + g // 2, (g % 2) * S + a * P:(g % 2) * S + (a + 1) * P], blk, ident)
                            if g % 2:
                                last.then_inc(kcvc_t, 1)
                    project(0, 2)
                    transpose_roped(0, 0)
                    transpose_roped(0, 1)
                    project(0, 3)
                    pe.wait_ge(cmpw_in, 32)
                    pe.wait_ge(stat_done, 8)
                    for m in range(CL // 2):
                        for w in range(2):
                            last = mm(ps[64 * w:64 * w + G * NC, 6, 0:CH], stat_kv[w][:, m].rearrange("p g n -> p (g n)"),
                                      ring[:, 4 + w, m * CH:(m + 1) * CH], start=(m == 0), stop=(m == CL // 2 - 1))
                    last.then_inc(cmpw_used, 1)
                    transpose_roped(0, 2)
                    transpose_roped(0, 3)
                    project(0, 4)
                    transpose_roped(0, 4)
                    transpose_roped(0, 5)
                    pe.wait_ge(gelu, 2)
                    for k in range(2):
                        last = tp(ps[:, 7, k * P:(k + 1) * P], hg[:, k * P:(k + 1) * P], ident)
                    last.then_inc(hg_t, 1)
                    pe.wait_ge(L.rope_mul, B.rope_mul + ropes(0, 6))
                    pe.wait_ge(w_lo, GATES + 1)
                    for a in range(T):
                        for j in range(KJ):
                            for k, (xs, ws) in enumerate(((xh, wh), (xh, wl), (xl, wh))):
                                cols = ws[:, GATES % WBUF, j * 3 * H:(j + 1) * 3 * H]
                                last = mm(ps[:, 10 % 4, a * 64:a * 64 + 3 * H], xs[:, j, a * P:(a + 1) * P], cols,
                                          start=(j == 0 and k == 0), stop=(j == KJ - 1 and k == 2))
                    last.then_inc(L.proj, 1)
                    pe.wait_ge(hgt_sb, 1)
                    pe.wait_ge(s_in, 112)
                    for w in range(2):
                        for k in range(2):
                            last = mm(ps[0:G * NC, 6, w * DH:(w + 1) * DH], hgT[:, k, 64 * w:64 * w + G * NC],
                                      w2[:, w, k, :], start=(k == 0), stop=(k == 1))
                    last.then_inc(w2_done, 1)
                    transpose_roped(0, 6)
                    transpose_roped(0, 7)
                    pe.wait_ge(kc_add, 1)
                    tp(ps[:, 7, 256:256 + G * NC], kcr[0:G * NC, :], ident[0:G * NC, 0:G * NC]).then_inc(kct, 1)
                else:
                    for r in range(0, 8, 2):
                        transpose_roped(1, r)
                        transpose_roped(1, r + 1)
                        project(1, 2 + r // 2)
                attention(l)
                mix_out(l)
                transpose_tile(0, R.xt, lambda w: pe.wait_ge(N.x_ready, ready(2 * l, 0, w)))
                logits(l, 0)
                for w in range(2):
                    seed(0, w, True)
                transpose_tile(1, R.xt, lambda w: pe.wait_ge(N.x_ready, ready(2 * l, 1, w)))
                logits(l, 1).then_inc(R.logits, 1)
                seed(1, 0, True)
                pe.wait_ge(R.sel, C.sel + 1)
                before, ones = const("before"), const("ones")
                mm(ps[:, 1, 0:E], before, sel[:, 0], start=True, stop=True)
                mm(ps[:, 1, E:2 * E], ones, sel[:, 0], start=True, stop=False)
                mm(ps[:, 1, E:2 * E], before, sel[:, 1], start=False, stop=True)
                mm(ps[0:1, 1, 2 * E:3 * E], ones[:, 0:1], sel[:, 0], start=True, stop=False)
                mm(ps[0:1, 1, 2 * E:3 * E], ones[:, 0:1], sel[:, 1], start=False, stop=True).then_inc(R.pos, 1)
                seed(1, 1, True)
                pe.wait_ge(R.xp, C.xp + T)
                round_(main, l)
                pe.wait_ge(R.over, C.over + 1)
                most = pe.value_load(over[0:1, 0:1], min_val=0, max_val=S)
                with pe.If(most > SLOTS):
                    with pe.Fori(0, ROUNDS - 1) as rho:
                        round_(rounds[1 + l], rho)

        @block.scalar
        def _(act):
            copy = nc.scalar.copy

            def transposed(dst, a, signal, at, done):
                act.wait_ge(signal, at + 2 * a + 1)
                copy(dst[:, 0:4, a * P:(a + 1) * P], ps[:, 2 * a, :].rearrange("p (j t) -> p j t", j=4)).then_inc(done, 1)

            def split_hi(u, j):
                c = chunk(u, j)
                if j % 4 == 0:
                    act.wait_ge(*AREA_IN(u, j // 4))
                wait_buffer(act, c)
                copy(wh[:, c % WBUF], area[:, j // 4, j % 4]).then_inc(w_hi, 1)

            def tr_copy(l, r):
                B = base[l]
                act.wait_ge(L.tr, B.tr + r + 1)
                a = r % 2
                if l == 0 and r < 4:
                    dst, n = kT[:, 2 * (r // 2):2 * (r // 2) + 2, a * P:(a + 1) * P], 2
                elif l == 0:
                    dst, n = qT[:, 4 * (r // 2 - 2):4 * (r // 2 - 1), a * P:(a + 1) * P], 4
                else:
                    d = qT if r < 4 else kT
                    dst, n = d[:, 4 * (r // 2 % 2):4 * (r // 2 % 2) + 4, a * P:(a + 1) * P], 4
                copy(dst, ps[:, 4 + r % 2, 0:n * P].rearrange("p (b t) -> p b t", b=n)).then_inc(L.tr_copied, 1)

            def round_(rd, rho):
                act.wait_ge(rd.gathered, (PAIRS + 1) * rho + 1)
                copy(XeT[:, 0:4, :], ps[:, 2, :].rearrange("p (j c) -> p j c", j=4)).then_inc(rd.xe, 1)
                with act.Fori(0, PAIRS) as i:
                    n, g = PAIRS * rho + i, (PAIRS + 1) * rho + i
                    act.wait_ge(rd.gate_done, n + 1)
                    nc.scalar.activation(sg, ps[:, 0, :], ACT.Silu).then_inc(rd.silu, 1)
                    act.wait_ge(rd.gathered, g + 2)
                    copy(XeT[:, 0:4, :], ps[:, 2, :].rearrange("p (j c) -> p j c", j=4)).then_inc(rd.xe, 1)
                    act.wait_ge(rd.gt, n + 1)
                    copy(GT, ps[:, 1, 0:2 * P].rearrange("p (a c) -> p a c", a=T)).then_inc(rd.gt_copied, 1)
                    act.wait_ge(rd.y, 2 * n + 2)
                    copy(Y[:, UNIT:2 * UNIT], ps[:, 3, :]).then_inc(rd.y_a, 1)

            for l in range(2):
                B, C = base[l], rbase[l]
                for n in range(4):
                    act.wait_ge(L.xt, B.xt + n + 1)
                    a, w = divmod(n, 2)
                    copy(xh[:, 4 * w:4 * w + 4, a * P:(a + 1) * P], ps[:, n, :].rearrange("p (j t) -> p j t", j=4)
                         ).then_inc(L.xh, 1)
                if l == 0:
                    for i in range(5):
                        for j in range(KJ):
                            split_hi(i, j)
                            if i == 1 and j in (1, 3):
                                n = j // 2
                                act.wait_ge(L.proj, B.proj + n + 1)
                                copy(raw[:, n], bc(ps[:, n, :].rearrange("p (g c) -> p g c", g=2 * G), 2, 2)).then_inc(L.copied, 1)
                            if i == 4 and j == 6:
                                act.wait_ge(cmpw_used, 1)
                                act.wait_ge(hg_zero, 1)
                                for w in range(2):
                                    r = slice(64 * w, 64 * w + G * NC)
                                    nc.scalar.activation(hg[r, :], ps[r, 6, 0:CH], ACT.Gelu_apprx_tanh).then_inc(gelu, 1)
                            if i in (2, 3) and j in (4, 7):
                                n = 2 * (i - 1) + j // 7
                                act.wait_ge(L.proj, B.proj + n + 1)
                                act.wait_ge(L.rope_mul, n - 1)
                                c = 256 * (n // 2 - 1)
                                copy(V[0][:, n % 2, c:c + 256], ps[:, n % 4, 256:512]).then_inc(L.copied, 1)
                            if i in (3, 4) and j in (1, 2):
                                tr_copy(0, 2 * (i - 3) + j - 1)
                    wait_buffer(act, GATES)
                    act.wait_ge(s_in, 112)
                    copy(wh[:, GATES % WBUF, 0:KJ * 3 * H], wgt[:, :, :].rearrange("p j c -> p (j c)")).then_inc(w_hi, 1)
                    tr_copy(0, 4)
                    tr_copy(0, 5)
                    act.wait_ge(hg_t, 1)
                    copy(hgT, ps[:, 7, 0:2 * P].rearrange("p (k c) -> p k c", k=2)).then_inc(hgt_sb, 1)
                    act.wait_ge(L.proj, B.proj + 11)
                    nc.scalar.activation(gates, ps[:, 2, 0:128].rearrange("p (a h) -> p a h", a=T)[:, :, 0:3 * H],
                                         ACT.Sigmoid).then_inc(L.copied, 1)
                    tr_copy(0, 6)
                    tr_copy(0, 7)
                    act.wait_ge(kct, 1)
                    copy(kcT[:, 0:G * NC], ps[:, 7, 256:256 + G * NC]).then_inc(kct_sb, 1)
                else:
                    def values(c):
                        act.wait_ge(L.proj, B.proj + 9 + c)
                        copy(V[1][:, c % 2, (c // 2) * UNIT:(c // 2 + 1) * UNIT], ps[:, c % 4, :]).then_inc(L.copied, 1)

                    for i in range(6):
                        for j in range(KJ):
                            split_hi(7 + i, j)
                            if i >= 2 and j in (1, 2):
                                tr_copy(1, 2 * (i - 2) + j - 1)
                            if i == 5 and j in (4, 6):
                                values(j // 2 - 2)
                    values(2)
                    values(3)

                n = len(ITEMS[l])
                for m in range(n + 2):
                    if m < n:
                        br = ITEMS[l][m][1]
                        act.wait_ge(L.mx, B.mx + m + 1)
                        if m >= 3:
                            act.wait_ge(L.pt, B.pt + m - 2)
                        for t in range(T):
                            for a in range(2):
                                if br:
                                    c, w = t * P, (t + 1) * P
                                    to = Pb[m % 3][:, 384 * a + c:384 * a + c + w]
                                else:
                                    c, w = t * DH, DH
                                    to = Pb[m % 3][:, (2 * t + a) * DH:(2 * t + a + 1) * DH]
                                last = nc.scalar.activation(to, ps[:, 2 * (m % 2) + a, c:c + w], ACT.Exp,
                                                            bias=nmax[:, m % 2, t, a:a + 1],
                                                            accum_out=sums[:, m % 3, t, a:a + 1])
                        last.then_inc(L.exp, 1)
                    if m >= 2:
                        act.wait_ge(L.pt, B.pt + m - 1)
                        w = 384 if ITEMS[l][m - 2][1] else P
                        copy(PTb[m % 2][:, 1, 0:w], ps[:, 5, 0:w]).then_inc(L.pt_sb, 1)
                permuted = lambda a: nc.scalar.copy(Xp[:, a], X[:, a].rearrange("p (c j) -> p j c", j=KJ)).then_inc(R.xp, 1)
                transposed(xTr, 0, R.xt, C.xt, R.xt_sb)
                act.wait_ge(N.x_ready, ready(2 * l, 0, 1))
                permuted(0)
                transposed(xTr, 1, R.xt, C.xt, R.xt_sb)
                act.wait_ge(R.logits, C.logits + 1)
                nc.scalar.activation(sc, ps[:, 0, 0:T * E].rearrange("p (a e) -> p a e", a=T), ACT.Sigmoid).then_inc(R.score, 1)
                act.wait_ge(N.x_ready, ready(2 * l, 1, 1))
                permuted(1)
                round_(main, l)
                act.wait_ge(R.over, C.over + 1)
                most = act.value_load(over[0:1, 0:1], min_val=0, max_val=S)
                with act.If(most > SLOTS):
                    act.wait_ge(main.comb, T * PAIRS * (l + 1))
                    with act.Fori(0, ROUNDS - 1) as rho:
                        round_(rounds[1 + l], rho)
                        act.wait_ge(rounds[1 + l].comb, T * PAIRS * (rho + 1))
                        act.sem_inc(round_over, 1)

        @block.gpsimd
        def _(pool):
            tt = nc.gpsimd.tensor_tensor
            steps = [0]

            def step(ins):
                steps[0] += 1
                ins.then_inc(pool_step, 1)
                pool.wait_ge(pool_step, steps[0])

            def round_(rd, rho):
                one_hot = Pm.rearrange("p a e c -> p (a e) c")
                g0 = (PAIRS + 1) * rho
                pool.wait_ge(rd.onehot, g0 + 1)
                gp_of = lambda i: bc(gate[:, :, bass.ds(2 * i, 2)] if not isinstance(i, int) else gate[:, :, 2 * i:2 * i + 2], 3, SLOTS)
                tt(GP, Pm, gp_of(0), ALU.mult).then_inc(rd.gp, 1)
                with pool.Fori(0, PAIRS) as i:
                    n, g = PAIRS * rho + i, g0 + i
                    pool.wait_ge(rd.onehot, g + 2)
                    pool.wait_ge(rd.gt, n + 1)
                    tt(GP, Pm, gp_of(i + 1), ALU.mult).then_inc(rd.gp, 1)

            nc.gpsimd.memset(hg, 0.0).then_inc(hg_zero, 1)
            step(nc.gpsimd.memset(kcT, 0.0))
            step(nc.gpsimd.memset(vc, 0.0))
            nc.gpsimd.memset(pos, -1.0)
            nc.gpsimd.memset(half, -0.5)
            step(nc.gpsimd.memset(gate, 0.0))
            pool.sem_inc(padded, 1)
            for l in range(2):
                B, C = base[l], rbase[l]
                for r in range(8):
                    pool.wait_ge(L.rope_mul, B.rope_mul + r + 1)
                    n = 256 if l == 0 and r < 4 else UNIT
                    tt(stage[r % 2][:, 0:n], stage[r % 2][:, 0:n], rope_b[r % 2][:, 0:n], ALU.add).then_inc(L.roped, 1)
                    if l == 0 and r == 7:
                        pool.wait_ge(kc_rope, 1)
                        n = G * NC
                        tt(kcr[0:n, :].rearrange("p (u c) -> p u c", u=2), bc(kca[0:n, :], 1, 2), bc(kcb[0:n, :], 1, 2),
                           ALU.add).then_inc(kc_add, 1)
                for m in range(len(ITEMS[l])):
                    pool.wait_ge(L.coef, B.coef + m + 1)
                    c = coef[:, m % 3]
                    if ITEMS[l][m][1]:
                        p3 = Pb[m % 3].rearrange("p (a k) -> p a k", a=2)
                        tt(p3[:, :, 0:P], p3[:, :, 0:P], bc(c[:, 0], 2, P), ALU.mult)
                        last = tt(p3[:, :, P:3 * P], p3[:, :, P:3 * P], bc(c[:, 1], 2, 2 * P), ALU.mult)
                    else:
                        p4 = Pb[m % 3][:, 0:4 * DH].rearrange("p (t a k) -> p t a k", t=T, a=2)
                        last = tt(p4, p4, bc(c, 3, DH), ALU.mult)
                    last.then_inc(L.scaled, 1)
                for k in (2 * l, 2 * l + 1):
                    for t in range(T):
                        pool.wait_ge(N.stats, k * T + t + 1)
                        tt(rstd[:, t:t + 1], ve[:, t:t + 1], half[:, t:t + 1], ALU.pow).then_inc(N.rstd, 1)
                    if k == 2 * l:
                        pool.wait_ge(R.table, C.table + 1)
                        round_(main, l)
                        pool.wait_ge(R.over, C.over + 1)
                        most = pool.value_load(over[0:1, 0:1], min_val=0, max_val=S)
                        with pool.If(most > SLOTS):
                            pool.wait_ge(main.comb, T * PAIRS * (l + 1))
                            pool.wait_ge(main.gp, (PAIRS + 1) * (l + 1))
                            with pool.Fori(0, ROUNDS - 1) as rho:
                                round_(rounds[1 + l], rho)
                                pool.wait_ge(rounds[1 + l].comb, T * PAIRS * (rho + 1))
                                pool.wait_ge(rounds[1 + l].gp, (PAIRS + 1) * (rho + 1))
                                pool.sem_inc(round_over, 1)

        @block.vector
        def _(dve):
            tt, ts, copy = nc.vector.tensor_tensor, nc.vector.tensor_scalar, nc.vector.tensor_copy
            stt = nc.vector.scalar_tensor_tensor
            steps = [0]

            def step(ins):
                steps[0] += 1
                ins.then_inc(dve_step, 1)
                dve.wait_ge(dve_step, steps[0])

            def transposed(dst, a, signal, at, done):
                dve.wait_ge(signal, at + 2 * a + 2)
                copy(dst[:, 4:8, a * P:(a + 1) * P], ps[:, 2 * a + 1, :].rearrange("p (j t) -> p j t", j=4)).then_inc(done, 1)

            def mask_copies():
                dve.wait_ge(c_in, 32)
                copy(identb[:, :], ident).then_inc(bconst, 1)
                copy(causalb[:, :], const("causal")).then_inc(bconst, 1)
                copy(cmaskb[:, :, :, :], cmask.rearrange("p (t g k) -> p t g k", t=T, g=G)).then_inc(bconst, 1)

            def split_x(l, a):
                for w in range(2):
                    n = 2 * a + w
                    dve.wait_ge(L.xh, base[l].xh + n + 1)
                    j, t = slice(4 * w, 4 * w + 4), slice(a * P, (a + 1) * P)
                    tt(xl[:, j, t], ps[:, n, :].rearrange("p (j t) -> p j t", j=4), xh[:, j, t], ALU.subtract).then_inc(L.xt_sb, 1)

            def split_lo(u, j):
                c = chunk(u, j)
                dve.wait_ge(w_hi, c + 1)
                tt(wl[:, c % WBUF], area[:, j // 4, j % 4], wh[:, c % WBUF], ALU.subtract).then_inc(w_lo, 1)

            def windows(w, gp):
                dve.wait_ge(s_in, 112)
                dve.wait_ge(kcvc_t, 2 * w + gp + 1)
                for par in range(2):
                    h = slice(64 * par, 64 * par + 64)
                    src = ps[h, 4 + 2 * w + gp, :].rearrange("p (g n m) -> p g n m", g=2, m=2 * 8)
                    for half_ in range(2):
                        s4 = src[:, :, half_:half_ + NC, par:16:2]
                        d4 = stat_kv[w][h, 8 * half_:8 * half_ + 8, 2 * gp:2 * gp + 2, :].rearrange("p m g n -> p g n m")
                        pp = bc(bc(posT[h, w, 8 * half_:8 * half_ + 8], 1, NC), 1, 2)
                        last = tt(d4, s4, pp, ALU.add)
                    last.then_inc(stat_done, 1)

            def rope(l, r):
                B = base[l]
                n = ROPE0[l] + r
                dve.wait_ge(L.proj, B.proj + n + 1)
                if r >= 2:
                    dve.wait_ge(L.tr, B.tr + r - 1)
                a = n % 2
                isq = r >= 4 if l == 0 else r < 4
                nh = 4 if l == 0 and r < 4 else 8
                cos = const("cosq" if isq else "cosk")[:, a * DH:(a + 1) * DH]
                sin = const("sinq" if isq else "sink")[:, a * DH:(a + 1) * DH]
                src, to, to_b = ps[:, n % 4, 0:nh * DH], stage[r % 2][:, 0:nh * DH], rope_b[r % 2][:, 0:nh * DH]
                if l == 0 and nh == 8:
                    src = src.rearrange("p (a i c) -> p a i c", a=2, i=4)
                    to, to_b = (v.rearrange("p (i a c) -> p a i c", a=2, i=4) for v in (to, to_b))
                else:
                    src, to, to_b = (v.rearrange("p (h c) -> p h c", h=nh) for v in (src, to, to_b))
                rope_mul(src, to, to_b, cos, sin).then_inc(L.rope_mul, 1)

            def rope_mul(src, to, to_b, cos, sin):
                def like(v, m):
                    for n in src.shape[1:-1]:
                        v = v.unsqueeze(1)
                    return v.to_broadcast(list(src.shape[:-1]) + [m])
                tt(to, src, like(cos, DH), ALU.mult)
                tt(to_b[..., 0:32], src[..., 32:64], like(sin[:, 0:32], 32), ALU.mult)
                return tt(to_b[..., 32:64], src[..., 0:32], like(sin[:, 32:64], 32), ALU.mult)

            def attention_max(l, m):
                B = base[l]
                dve.wait_ge(L.s_done, B.s_done + m + 1)
                b = 2 * (m % 2)
                if ITEMS[l][m][1]:
                    for t in range(T):
                        last = nc.vector.tensor_reduce(nmax[:, m % 2, t, :], ps[:, b:b + 2, t * P:t * P + (t + 1) * P],
                                                       AX.X, ALU.max, negate=True)
                else:
                    last = nc.vector.tensor_reduce(nmax[:, m % 2].rearrange("p t a -> p a t"),
                                                   ps[:, b:b + 2, 0:2 * DH].rearrange("p a (t k) -> p a t k", t=T),
                                                   AX.X, ALU.max, negate=True)
                last.then_inc(L.mx, 1)

            def coefficients(l, m):
                B = base[l]
                jq, br, _, _ = ITEMS[l][m]
                dve.wait_ge(L.exp, B.exp + m + 1)
                if m >= 3:
                    dve.wait_ge(L.scaled, B.scaled + m - 2)
                c = coef[:, m % 3]
                last = nc.vector.reciprocal(c, sums[:, m % 3])
                if l == 0:
                    step(last)
                    h0 = 8 * (jq // 4) + jq % 4
                    g = gates[:, :, br * H:(br + 1) * H].rearrange("p t (u i) -> p t u i", i=4)
                    last = tt(c, c, g[:, :, h0 // 4:h0 // 4 + 2, h0 % 4], ALU.mult)
                last.then_inc(L.coef, 1)

            def layer_norm(k, t, signal, counts, ln_in, ln_n):
                for w in range(2):
                    dve.wait_ge(signal, counts[w])
                    last = nc.vector.bn_stats(bst[:, t, w, :], ps[:, 4 + 2 * t + w, :])
                step(last)
                step(nc.vector.bn_aggr(mv[:, t], bst[:, t].rearrange("p w s -> p (w s)")))
                ts(ve[:, t:t + 1], mv[:, t, 1:2], EPS, None, ALU.add).then_inc(N.stats, 1)
                dve.wait_ge(ln_in, ln_n)
                for w in range(2):
                    c = slice(w * UNIT, (w + 1) * UNIT)
                    last = stt(X[:, t, c], ps[:, 4 + 2 * t + w, :], mv[:, t, 0:1], lnw[:, 0, c], ALU.subtract, ALU.mult)
                    if w == 0:
                        first = steps[0] = steps[0] + 1
                    else:
                        steps[0] += 1
                    last.then_inc(dve_step, 1)
                dve.wait_ge(N.rstd, k * T + t + 1)
                for w in range(2):
                    c = slice(w * UNIT, (w + 1) * UNIT)
                    dve.wait_ge(dve_step, first + w)
                    stt(X[:, t, c], X[:, t, c], rstd[:, t:t + 1], lnw[:, 1, c], ALU.mult, ALU.add).then_inc(N.x_ready, 1)

            def ranks(v, n, out_):
                c1 = cg[:, 0:n * EG * EG].rearrange("p (g i j) -> p g i j", i=EG, j=EG)
                c2 = ch[:, 0:n * EG * EG].rearrange("p (g i j) -> p g i j", i=EG, j=EG)
                other, own = bc(v, 2, EG), bc(v, 3, EG)
                low = bc(const("lower").rearrange("p (i j) -> p i j", i=EG), 1, n)
                tt(c1, other, own, ALU.is_gt)
                step(tt(c2, other, own, ALU.is_ge))
                step(tt(c2, c2, low, ALU.mult))
                step(tt(c1, c1, c2, ALU.max))
                step(nc.vector.tensor_reduce(out_, c1, AX.X, ALU.add))

            def routing(C):
                dve.wait_ge(R.score, C.score + 1)
                dve.wait_ge(s_in, 112)
                step(tt(bs, sc, bc(rb, 1, T), ALU.add))
                b3 = bs.rearrange("p a (g e) -> p (a g) e", e=EG)
                r3 = rank[:, :].rearrange("p (g e) -> p g e", e=EG)
                s3 = sel2[:, :].rearrange("p (g e) -> p g e", e=EG)
                ranks(b3, T * EG, r3)
                step(ts(s3, r3, 1.5, None, ALU.is_lt))
                c3 = ch[:, 0:T * E].rearrange("p (g e) -> p g e", e=EG)
                step(tt(c3, b3, s3, ALU.mult))
                step(nc.vector.tensor_reduce(gs, c3, AX.X, ALU.add))
                ranks(gs[:, :].rearrange("p (a g) -> p a g", a=T), T, rank[:, 0:T * EG].rearrange("p (a g) -> p a g", a=T))
                step(ts(gsel, rank[:, 0:T * EG], 0.5, None, ALU.is_lt))
                f = sel.rearrange("p a (g e) -> p (a g) e", e=EG)
                tt(f, s3, bc(gsel, 2, EG), ALU.mult).then_inc(R.sel, 1)
                dve.wait_ge(R.sel, C.sel + 1)
                w = ch[:, 0:T * E].rearrange("p (a e) -> p a e", a=T)
                step(tt(w, sc, sel, ALU.mult))
                step(nc.vector.tensor_reduce(wsum, w, AX.X, ALU.add))
                step(nc.vector.reciprocal(wsum, wsum))
                dve.wait_ge(padded, 1)
                step(tt(gate[:, :, 0:E], w, bc(wsum, 2, E), ALU.mult))
                dve.wait_ge(R.pos, C.pos + 1)
                nc.vector.tensor_reduce(over[0:1, 0:1], ps[0:1, 1, 2 * E:3 * E], AX.X, ALU.max).then_inc(R.over, 1)
                step(nc.vector.scalar_tensor_tensor(pos[:, :, 0:E], ps[:, 1, 0:T * E].rearrange("p (a e) -> p a e", a=T), 1.0,
                                                    sel, ALU.add, ALU.mult))
                ts(pos[:, :, 0:E], pos[:, :, 0:E], -1.0, None, ALU.add).then_inc(R.table, 1)
                dve.wait_ge(R.table, C.table + 1)

            def one_hot(i):
                src = pos[:, :, bass.ds(2 * i, 2)] if not isinstance(i, int) else pos[:, :, 2 * i:2 * i + 2]
                return tt(Pm, bc(bc(const("slot"), 1, 2), 1, T), bc(src, 3, SLOTS), ALU.is_equal)

            def round_(rd, rho, shift):
                g0 = (PAIRS + 1) * rho
                if shift:
                    ts(pos, pos, float(-SLOTS), None, ALU.add).then_inc(rd.shift, 1)
                    dve.wait_ge(rd.shift, rho + 1)
                one_hot(0).then_inc(rd.onehot, 1)
                dve.wait_ge(rd.gathered, g0 + 1)
                copy(XeT[:, 4:8, :], ps[:, 3, :].rearrange("p (j c) -> p j c", j=4)).then_inc(rd.xe, 1)
                with dve.Fori(0, PAIRS) as i:
                    n, g = PAIRS * rho + i, g0 + i
                    dve.wait_ge(rd.gp, g + 1)
                    dve.wait_ge(rd.gathered, g + 1)
                    one_hot(i + 1).then_inc(rd.onehot, 1)
                    dve.wait_ge(rd.silu, n + 1)
                    dve.wait_ge(rd.up_done, n + 1)
                    tt(hid, sg, ps[:, 1, :], ALU.mult).then_inc(rd.h, 1)
                    dve.wait_ge(rd.gathered, g + 2)
                    copy(XeT[:, 4:8, :], ps[:, 3, :].rearrange("p (j c) -> p j c", j=4)).then_inc(rd.xe, 1)
                    dve.wait_ge(rd.ht, n + 1)
                    copy(hT, ps[:, 0, :].rearrange("p (k c) -> p k c", k=FJ)).then_inc(rd.ht_sb, 1)
                    dve.wait_ge(rd.y, 2 * n + 1)
                    copy(Y[:, 0:UNIT], ps[:, 2, :]).then_inc(rd.y_d, 1)

            for l in range(2):
                B, C = base[l], rbase[l]
                if l == 0:
                    for a in range(T):
                        split_x(0, a)
                    for i in range(5):
                        for j in range(KJ):
                            if i == 1 and j == 0:
                                mask_copies()
                            split_lo(i, j)
                            if i >= 2 and j in (2, 5):
                                rope(0, 2 * (i - 2) + j // 5)
                            if i in (2, 3) and j in (3, 6):
                                windows(i - 2, j // 6)
                    dve.wait_ge(w_hi, GATES + 1)
                    tt(wl[:, GATES % WBUF, 0:KJ * 3 * H], wgt[:, :, :].rearrange("p j c -> p (j c)"),
                       wh[:, GATES % WBUF, 0:KJ * 3 * H], ALU.subtract).then_inc(w_lo, 1)
                    for r in (6, 7):
                        rope(0, r)
                    dve.wait_ge(w2_done, 1)
                    n = G * NC
                    rope_mul(ps[0:n, 6, 0:DH], kca[0:n, :], kcb[0:n, :], const("ccos")[0:n, :], const("csin")[0:n, :]
                             ).then_inc(kc_rope, 1)
                    dve.wait_ge(padded, 1)
                    copy(vc[0:n, :], ps[0:n, 6, DH:2 * DH])
                    copy(vc[64:64 + n, :], ps[0:n, 6, DH:2 * DH]).then_inc(vc_done, 1)
                    dve.wait_ge(L.copied, 7)
                    for t in range(T):
                        last = ts(gates[:, t, 0:H], gates[:, t, 0:H], const("valid")[:, t:t + 1], None, ALU.mult)
                    step(last)
                else:
                    for i in range(6):
                        for j in range(KJ):
                            split_lo(7 + i, j)
                            if 1 <= i <= 4 and j in (2, 5):
                                rope(1, 2 * (i - 1) + j // 5)
                n, nb = len(ITEMS[l]), BRANCHES[l]
                for m in range(n + 4):
                    if m < n:
                        attention_max(l, m)
                    if 1 <= m <= n:
                        coefficients(l, m - 1)
                    if 2 <= m < n + 2:
                        dve.wait_ge(L.pt, B.pt + m - 1)
                        w = 384 if ITEMS[l][m - 2][1] else P
                        copy(PTb[m % 2][:, 0, 0:w], ps[:, 4, 0:w]).then_inc(L.pt_sb, 1)
                    if m >= 4 and (m - 4) % nb == nb - 1:
                        dve.wait_ge(L.pv, B.pv + m - 3)
                        jq = (m - 4) // nb
                        copy(OT[jq], ps[:, 6 + jq % 2, 0:S]).then_inc(L.ot_sb, 1)
                for t in range(T):
                    layer_norm(2 * l, t, L.mix, [B.mix + t + 1, B.mix + t + 3], L.ln_in, B.ln_in + 32)
                    transposed(xTr, t, R.xt, C.xt, R.xt_sb)
                routing(C)
                round_(main, l, False)
                most = dve.value_load(over[0:1, 0:1], min_val=0, max_val=S)
                with dve.If(most > SLOTS):
                    dve.wait_ge(main.comb, T * PAIRS * (l + 1))
                    dve.wait_ge(main.gp, (PAIRS + 1) * (l + 1))
                    with dve.Fori(0, ROUNDS - 1) as rho:
                        round_(rounds[1 + l], rho, True)
                        dve.wait_ge(rounds[1 + l].comb, T * PAIRS * (rho + 1))
                        dve.wait_ge(rounds[1 + l].gp, (PAIRS + 1) * (rho + 1))
                        dve.sem_inc(round_over, 1)
                for t in range(T):
                    layer_norm(2 * l + 1, t, main.comb, [T * (PAIRS * (l + 1) - 1) + t + 1] * 2, R.ln_in, C.ln_in + 32)
                if l == 0:
                    for t in range(T):
                        split_x(1, t)


def kernel(**inputs):
    import concourse.bacc as bacc
    from concourse.bass_utils import run_bass_kernel_spmd

    a = {k: np.asarray(v) for k, v in inputs.items()}
    places = lambda p: np.ascontiguousarray(p[0].reshape(CL // 2, 2 * DH).T)
    beside = lambda w: w.reshape(2, 2, 4, DH, D).transpose(0, 2, 1, 3, 4).reshape(D, D)
    arrays = {
        "x": a["x"][0], "consts": constants(), "w_in0": a["nsa_w_in"][0], "w_out0": beside(a["nsa_w_out"][0]),
        "cmp_kw1": a["nsa_cmp_k_w1"][0], "cmp_kw2": a["nsa_cmp_k_w2"][0],
        "cmp_vw1": a["nsa_cmp_v_w1"][0], "cmp_vw2": a["nsa_cmp_v_w2"][0],
        "cmp_kpos": places(a["nsa_cmp_k_pos"]), "cmp_vpos": places(a["nsa_cmp_v_pos"]),
        "w_in1": a["moba_w_in"][0], "w_out1": a["moba_w_out"][0],
        "router_w": a["router_w"], "router_b": a["router_bias"].reshape(1, E),
        "w_gate": a["moe_w_gate"], "w_up": a["moe_w_up"], "w_down": a["moe_w_down"],
        "ln_g": a["ln_g"], "ln_b": a["ln_b"],
    }
    nc = bacc.Bacc("TRN2", target_bir_lowering=False, num_devices=1)
    feed, args = {}, []
    for name, v in arrays.items():
        v = np.ascontiguousarray(v)
        feed[f"in_{name}"] = v
        args.append(nc.dram_tensor(f"in_{name}", v.shape, mybir.dt.from_np(v.dtype), kind="ExternalInput").ap())
    args.append(nc.dram_tensor("out", (S, D), F32, kind="ExternalOutput").ap())
    build(nc, *args)
    r = run_bass_kernel_spmd(nc, [feed], core_ids=[0])
    return r.results[0]["out"].reshape(1, S, D)
```
